# Optimizing a Trainium2 kernel written in Bass

```python
import math
import jax, jax.numpy as jnp
from jax import lax
import numpy as np

D_MODEL = 1024
BATCH = 1
SEQ = 256
DEPTH = 2

RMS_EPS = 1e-6
ROPE_THETA = 10000.0
ATTN_Q_BLOCK = 128

MLA_HEADS = 4
MLA_NOPE_DIM = 128
MLA_ROPE_DIM = 64
MLA_V_DIM = 128
MLA_QK_DIM = MLA_NOPE_DIM + MLA_ROPE_DIM
MLA_Q_RANK = 384
MLA_KV_RANK = 256
MLA_WIDTH = MLA_HEADS * MLA_V_DIM

DN_HEADS = 4
DN_HEAD_DIM = 128
DN_WIDTH = DN_HEADS * DN_HEAD_DIM
DN_CONV = 4
DN_CHUNK = 64

DIL_WINDOWS = (128, 512, 2048)
DIL_DILATIONS = (1, 4, 16)
DIL_GROUPS = 3
DIL_HEADS_PER_GROUP = 4
DIL_HEAD_DIM = 128
DIL_QKV_WIDTH = DIL_GROUPS * DIL_HEADS_PER_GROUP * DIL_HEAD_DIM
DIL_WIDTH = DIL_HEADS_PER_GROUP * DIL_HEAD_DIM
DIL_BLOCK = 128

N_BRANCHES = 3
BRANCH_WIDTH = 512
IN_SPLITS = (MLA_Q_RANK, MLA_KV_RANK + MLA_ROPE_DIM, MLA_WIDTH,
             3 * DN_WIDTH, DN_HEADS, DN_HEADS, DN_WIDTH,
             3 * DIL_QKV_WIDTH, DIL_WIDTH,
             N_BRANCHES * D_MODEL)
IN_WIDTH = (MLA_Q_RANK + MLA_KV_RANK + MLA_ROPE_DIM + MLA_WIDTH
            + 3 * DN_WIDTH + 2 * DN_HEADS + DN_WIDTH
            + 3 * DIL_QKV_WIDTH + DIL_WIDTH + N_BRANCHES * D_MODEL)

kernel_name = "hybrid_mla_gdn_dilated_gated_merge"

def rms_norm(x, g):
    xf = x.astype(jnp.float32)
    y = xf * lax.rsqrt(jnp.mean(xf * xf, axis=-1, keepdims=True) + RMS_EPS)
    return (y * g.astype(jnp.float32)).astype(x.dtype)

def l2_normalize(x):
    return x * lax.rsqrt(jnp.sum(x * x, axis=-1, keepdims=True) + 1e-6)

def rope_tables(positions, dim):
    inv_freq = 1.0 / (ROPE_THETA ** (jnp.arange(0, dim, 2, dtype=jnp.float32) / dim))
    ang = positions.astype(jnp.float32)[..., None] * inv_freq
    return jnp.cos(ang), jnp.sin(ang)

def apply_rope(x, cos, sin):
    half = x.shape[-1] // 2
    xf = x.astype(jnp.float32)
    x1, x2 = xf[..., :half], xf[..., half:]
    c, s = cos[:, :, None, :], sin[:, :, None, :]
    return jnp.concatenate([x1 * c - x2 * s, x2 * c + x1 * s], axis=-1).astype(x.dtype)

def split_last(t, sizes):
    cuts, acc = [], 0
    for size in sizes[:-1]:
        acc += size
        cuts.append(acc)
    return jnp.split(t, cuts, axis=-1)

def causal_depthwise_conv(x, w):
    k = w.shape[0]
    return lax.conv_general_dilated(
        x, w[:, None, :].astype(x.dtype), window_strides=(1,), padding=[(k - 1, 0)],
        dimension_numbers=('NWC', 'WIO', 'NWC'), feature_group_count=x.shape[-1])

def causal_block_attention(q, k, v, scale):
    B, S, H, dk = q.shape
    dv = v.shape[-1]
    nb = S // ATTN_Q_BLOCK
    q_blocks = jnp.moveaxis(q.reshape(B, nb, ATTN_Q_BLOCK, H, dk), 1, 0)
    k_pos = jnp.arange(S)

    def one_block(args):
        q_blk, blk = args
        s = jnp.einsum('bqhd,bkhd->bhqk', q_blk, k, preferred_element_type=jnp.float32) * scale
        q_pos = blk * ATTN_Q_BLOCK + jnp.arange(ATTN_Q_BLOCK)
        s = jnp.where(k_pos[None, :] <= q_pos[:, None], s, -jnp.inf)
        p = jax.nn.softmax(s, axis=-1)
        return jnp.einsum('bhqk,bkhd->bqhd', p.astype(v.dtype), v)

    o = lax.map(one_block, (q_blocks, jnp.arange(nb)))
    return jnp.moveaxis(o, 0, 1).reshape(B, S, H, dv)

def mla_branch(q_lat, kv_lat, cos, sin, q_a_norm_g, w_q_b, kv_a_norm_g, w_kv_b, q_norm_g, k_norm_g):
    B, S, _ = q_lat.shape
    q = jnp.einsum('bsr,re->bse', rms_norm(q_lat, q_a_norm_g), w_q_b).reshape(B, S, MLA_HEADS, MLA_QK_DIM)
    c_kv, k_pe = kv_lat[..., :MLA_KV_RANK], kv_lat[..., MLA_KV_RANK:]
    kv = jnp.einsum('bsr,re->bse', rms_norm(c_kv, kv_a_norm_g), w_kv_b).reshape(B, S, MLA_HEADS, MLA_NOPE_DIM + MLA_V_DIM)
    k_nope, v = kv[..., :MLA_NOPE_DIM], kv[..., MLA_NOPE_DIM:]
    q_nope = rms_norm(q[..., :MLA_NOPE_DIM], q_norm_g[:MLA_NOPE_DIM])
    q_pe = apply_rope(rms_norm(q[..., MLA_NOPE_DIM:], q_norm_g[MLA_NOPE_DIM:]), cos, sin)
    k_nope = rms_norm(k_nope, k_norm_g[:MLA_NOPE_DIM])
    k_pe = apply_rope(rms_norm(k_pe, k_norm_g[MLA_NOPE_DIM:])[:, :, None, :], cos, sin)
    q_full = jnp.concatenate([q_nope, q_pe], axis=-1)
    k_full = jnp.concatenate([k_nope, jnp.broadcast_to(k_pe, (B, S, MLA_HEADS, MLA_ROPE_DIM))], axis=-1)
    o = causal_block_attention(q_full, k_full, v, MLA_QK_DIM ** -0.5)
    return o.reshape(B, S, MLA_WIDTH)

def chunk_gated_delta_rule(q, k, v, g, beta):
    B, S, H, dk = q.shape
    dv = v.shape[-1]
    C = DN_CHUNK
    N = S // C

    def chunks(t):
        t = jnp.moveaxis(t, 2, 1)
        return t.reshape(B, H, N, C, *t.shape[3:])

    q, k, v, g, beta = (chunks(t) for t in (q, k, v, g, beta))
    gc = jnp.cumsum(g, axis=-1)
    idx = jnp.arange(C)
    incl = idx[:, None] >= idx[None, :]
    strict = idx[:, None] > idx[None, :]
    decay = jnp.exp(jnp.where(incl, gc[..., :, None] - gc[..., None, :], -jnp.inf))
    k_beta = k * beta[..., None]
    lower = jnp.where(strict, jnp.einsum('bhncd,bhnmd->bhncm', k_beta, k) * decay, 0.0)
    rhs = jnp.concatenate([v * beta[..., None], k_beta * jnp.exp(gc)[..., None]], axis=-1)
    sol = lax.linalg.triangular_solve(lower + jnp.eye(C, dtype=lower.dtype), rhs, left_side=True, lower=True)
    u, w = sol[..., :dv], sol[..., dv:]
    qk = jnp.einsum('bhncd,bhnmd->bhncm', q, k) * decay

    def step(state, inp):
        q_i, k_i, u_i, w_i, gc_i, qk_i = inp
        v_new = u_i - jnp.einsum('bhcd,bhde->bhce', w_i, state)
        o_i = (jnp.einsum('bhcd,bhde->bhce', q_i * jnp.exp(gc_i)[..., None], state)
               + jnp.einsum('bhcm,bhme->bhce', qk_i, v_new))
        g_last = gc_i[..., -1:]
        state = (state * jnp.exp(g_last)[..., None]
                 + jnp.einsum('bhcd,bhce->bhde', k_i * jnp.exp(g_last - gc_i)[..., None], v_new))
        return state, o_i

    xs = tuple(jnp.moveaxis(t, 2, 0) for t in (q, k, u, w, gc, qk))
    state0 = jnp.zeros((B, H, dk, dv), jnp.float32)
    _, o = lax.scan(step, state0, xs)
    o = jnp.moveaxis(o, 0, 2).reshape(B, H, S, dv)
    return jnp.moveaxis(o, 1, 2)

def gated_deltanet_branch(qkv, a, b, conv_w, a_log, dt_bias, out_norm_g):
    B, S, _ = qkv.shape
    mixed = jax.nn.silu(causal_depthwise_conv(qkv, conv_w)).astype(jnp.float32)
    q, k, v = jnp.split(mixed, 3, axis=-1)
    q = l2_normalize(q.reshape(B, S, DN_HEADS, DN_HEAD_DIM)) * (DN_HEAD_DIM ** -0.5)
    k = l2_normalize(k.reshape(B, S, DN_HEADS, DN_HEAD_DIM))
    v = v.reshape(B, S, DN_HEADS, DN_HEAD_DIM)
    beta = jax.nn.sigmoid(b.astype(jnp.float32))
    g = -jnp.exp(a_log.astype(jnp.float32)) * jax.nn.softplus(a.astype(jnp.float32) + dt_bias.astype(jnp.float32))
    o = chunk_gated_delta_rule(q, k, v, g, beta)
    return rms_norm(o, out_norm_g).astype(qkv.dtype).reshape(B, S, DN_WIDTH)

def dilated_window_attention(q, k, v, window, dilation):
    B, S, H, hd = q.shape
    reach = window // dilation
    L = S // dilation
    nb = -(-L // DIL_BLOCK)
    Lp = nb * DIL_BLOCK

    def to_blocks(t):
        t = jnp.swapaxes(t.reshape(B, L, dilation, H, hd), 1, 2)
        t = jnp.pad(t, ((0, 0), (0, 0), (0, Lp - L), (0, 0), (0, 0)))
        return t.reshape(B, dilation, nb, DIL_BLOCK, H, hd)

    def with_previous(t):
        prev = jnp.pad(t[:, :, :-1], ((0, 0), (0, 0), (1, 0), (0, 0), (0, 0), (0, 0)))
        return jnp.concatenate([prev, t], axis=3)

    qb = to_blocks(q)
    kb = with_previous(to_blocks(k))
    vb = with_previous(to_blocks(v))
    s = jnp.einsum('bgnqhd,bgnkhd->bgnhqk', qb, kb, preferred_element_type=jnp.float32) * (hd ** -0.5)
    qi = jnp.arange(DIL_BLOCK)[:, None]
    kc = jnp.arange(2 * DIL_BLOCK)[None, :]
    dist = DIL_BLOCK + qi - kc
    band = (dist >= 0) & (dist <= reach)
    has_prev = (jnp.arange(nb) > 0)[:, None, None] | (kc >= DIL_BLOCK)[None]
    valid = band[None] & has_prev
    s = jnp.where(valid[:, None], s, -jnp.inf)
    m = jnp.max(s, axis=-1, keepdims=True)
    e = jnp.exp(s - m)
    den = jnp.sum(e, axis=-1)
    o = jnp.einsum('bgnhqk,bgnkhd->bgnqhd', e, vb.astype(jnp.float32)) / jnp.swapaxes(den, -1, -2)[..., None]
    lse = jnp.swapaxes(m[..., 0] + jnp.log(den), -1, -2)

    def from_blocks(t):
        t = t.reshape(B, dilation, Lp, *t.shape[4:])[:, :, :L]
        return jnp.swapaxes(t, 1, 2).reshape(B, S, *t.shape[3:])

    return from_blocks(o), from_blocks(lse)

def dilated_branch(qkv, cos, sin, q_norm_g, k_norm_g):
    B, S, _ = qkv.shape
    n_heads = DIL_GROUPS * DIL_HEADS_PER_GROUP
    q, k, v = (t.reshape(B, S, n_heads, DIL_HEAD_DIM) for t in jnp.split(qkv, 3, axis=-1))
    q = apply_rope(rms_norm(q, q_norm_g), cos, sin)
    k = apply_rope(rms_norm(k, k_norm_g), cos, sin)
    grp = (B, S, DIL_GROUPS, DIL_HEADS_PER_GROUP, DIL_HEAD_DIM)
    q, k, v = q.reshape(grp), k.reshape(grp), v.reshape(grp)
    outs, lses = [], []
    for gi in range(DIL_GROUPS):
        o_g, lse_g = dilated_window_attention(q[:, :, gi], k[:, :, gi], v[:, :, gi], DIL_WINDOWS[gi], DIL_DILATIONS[gi])
        outs.append(o_g)
        lses.append(lse_g)
    wts = jax.nn.softmax(jnp.stack(lses, axis=0), axis=0)
    o = jnp.sum(wts[..., None] * jnp.stack(outs, axis=0), axis=0)
    return o.reshape(B, S, DIL_WIDTH).astype(qkv.dtype)

def hybrid_layer(x, cos_r, sin_r, cos_h, sin_h, norm_g, w_in, mla_q_a_norm_g, mla_w_q_b,
                 mla_kv_a_norm_g, mla_w_kv_b, mla_q_norm_g, mla_k_norm_g, dn_conv_w, dn_a_log,
                 dn_dt_bias, dn_out_norm_g, dil_q_norm_g, dil_k_norm_g, w_branch, w_out):
    B, S, _ = x.shape
    h = rms_norm(x, norm_g)
    proj = jnp.einsum('bsd,de->bse', h, w_in)
    (q_lat, kv_lat, z_a, dn_qkv, dn_a, dn_b, z_b, dil_qkv, z_c, gate_logits) = split_last(proj, IN_SPLITS)
    y_a = mla_branch(q_lat, kv_lat, cos_r, sin_r, mla_q_a_norm_g, mla_w_q_b, mla_kv_a_norm_g,
                     mla_w_kv_b, mla_q_norm_g, mla_k_norm_g)
    y_b = gated_deltanet_branch(dn_qkv, dn_a, dn_b, dn_conv_w, dn_a_log, dn_dt_bias, dn_out_norm_g)
    y_c = dilated_branch(dil_qkv, cos_h, sin_h, dil_q_norm_g, dil_k_norm_g)
    ys = jnp.stack([y_a * jax.nn.silu(z_a), y_b * jax.nn.silu(z_b), y_c * jax.nn.silu(z_c)], axis=2)
    branch_out = jnp.einsum('bsnc,ncd->bsnd', ys, w_branch)
    gates = jax.nn.sigmoid(gate_logits.reshape(B, S, N_BRANCHES, D_MODEL))
    mixed = jnp.sum(gates * branch_out, axis=2)
    return x + jnp.einsum('bsd,de->bse', mixed, w_out)

def setup_inputs(seed: int = 0) -> dict:
    key = jax.random.key(seed)
    ks = jax.random.split(key, 24)
    f32 = jnp.float32

    def normal(k, shape, fan_in):
        return jax.random.normal(k, shape, f32) * (fan_in ** -0.5)

    def gain(k, shape):
        return 1.0 + 0.02 * jax.random.normal(k, shape, f32)

    x = jax.random.normal(ks[0], (BATCH, SEQ, D_MODEL), f32)
    offsets = jax.random.randint(ks[1], (BATCH, 1), 0, 1024, dtype=jnp.int32)
    positions = jnp.arange(SEQ, dtype=jnp.int32)[None, :] + offsets
    dt = jnp.exp(jax.random.uniform(ks[14], (DEPTH, DN_HEADS), f32, math.log(1e-3), math.log(1e-1)))
    return {
        "x": x,
        "positions": positions,
        "norm_g": gain(ks[2], (DEPTH, D_MODEL)),
        "w_in": normal(ks[3], (DEPTH, D_MODEL, IN_WIDTH), D_MODEL),
        "mla_q_a_norm_g": gain(ks[4], (DEPTH, MLA_Q_RANK)),
        "mla_w_q_b": normal(ks[5], (DEPTH, MLA_Q_RANK, MLA_HEADS * MLA_QK_DIM), MLA_Q_RANK),
        "mla_kv_a_norm_g": gain(ks[6], (DEPTH, MLA_KV_RANK)),
        "mla_w_kv_b": normal(ks[7], (DEPTH, MLA_KV_RANK, MLA_HEADS * (MLA_NOPE_DIM + MLA_V_DIM)), MLA_KV_RANK),
        "mla_q_norm_g": gain(ks[8], (DEPTH, MLA_QK_DIM)),
        "mla_k_norm_g": gain(ks[9], (DEPTH, MLA_QK_DIM)),
        "dn_conv_w": normal(ks[10], (DEPTH, DN_CONV, 3 * DN_WIDTH), DN_CONV),
        "dn_a_log": jnp.log(jax.random.uniform(ks[11], (DEPTH, DN_HEADS), f32, 1.0, 16.0)),
        "dn_dt_bias": dt + jnp.log(-jnp.expm1(-dt)),
        "dn_out_norm_g": gain(ks[12], (DEPTH, DN_HEAD_DIM)),
        "dil_q_norm_g": gain(ks[13], (DEPTH, DIL_HEAD_DIM)),
        "dil_k_norm_g": gain(ks[15], (DEPTH, DIL_HEAD_DIM)),
        "w_branch": normal(ks[16], (DEPTH, N_BRANCHES, BRANCH_WIDTH, D_MODEL), BRANCH_WIDTH),
        "w_out": normal(ks[17], (DEPTH, D_MODEL, D_MODEL), D_MODEL),
    }

def reference(x, positions, norm_g, w_in, mla_q_a_norm_g, mla_w_q_b, mla_kv_a_norm_g, mla_w_kv_b,
              mla_q_norm_g, mla_k_norm_g, dn_conv_w, dn_a_log, dn_dt_bias, dn_out_norm_g,
              dil_q_norm_g, dil_k_norm_g, w_branch, w_out):
    cos_r, sin_r = rope_tables(positions, MLA_ROPE_DIM)
    cos_h, sin_h = rope_tables(positions, DIL_HEAD_DIM)
    for layer in range(DEPTH):
        x = hybrid_layer(x, cos_r, sin_r, cos_h, sin_h, norm_g[layer], w_in[layer],
                         mla_q_a_norm_g[layer], mla_w_q_b[layer], mla_kv_a_norm_g[layer],
                         mla_w_kv_b[layer], mla_q_norm_g[layer], mla_k_norm_g[layer],
                         dn_conv_w[layer], dn_a_log[layer], dn_dt_bias[layer], dn_out_norm_g[layer],
                         dil_q_norm_g[layer], dil_k_norm_g[layer], w_branch[layer], w_out[layer])
    return x


_drawn_inputs = setup_inputs


def setup_inputs(seed=0):
    import zlib

    import numpy as np

    out = dict(_drawn_inputs(seed))
    spreads = {}
    factors = {'norm_g': 3.564,
     'mla_q_a_norm_g': 8.0,
     'mla_kv_a_norm_g': 8.0,
     'mla_q_norm_g': 8.0,
     'mla_k_norm_g': 8.0,
     'dn_out_norm_g': 6.846,
     'dil_q_norm_g': 8.0,
     'dil_k_norm_g': 8.0}
    for name, (base, spread) in spreads.items():
        noise = np.random.default_rng([zlib.crc32(name.encode()), seed]).standard_normal(out[name].shape)
        drawn = base * np.exp(spread * noise) if base else spread * noise
        out[name] = __import__('jax').numpy.asarray(drawn.astype(out[name].dtype))
    for name, factor in factors.items():
        out[name] = (out[name] * factor).astype(out[name].dtype)
    return out
```

```python
from contextlib import ExitStack

import numpy as np

import concourse.bass as bass
from concourse import mybir

ALU = mybir.AluOpType
ACT = mybir.ActivationFunctionType
AX = mybir.AxisListType
F32 = mybir.dt.float32
F32R = mybir.dt.float32r
I32 = mybir.dt.int32

P = 128
NT = 2
S = NT * P
D = 1024
KC = D // P
H = 4
HD = 128
W = H * HD
CH = 64
DEPTH = 2
EPS = 1e-6
NEG = -1e30
Q_RANK, KV_RANK, ROPE = 384, 256, 64
QK = HD + ROPE
CONV = 4
GROUPS = 3
DILATIONS = (1, 4, 16)
BRANCHES = 3
LEVELS = (1, 2, 4, 8, 16, 32)
PIECES = 2

COL, _at = {}, 0
for _name, _n in (("q_lat", Q_RANK), ("kv_lat", KV_RANK + ROPE), ("z0", W), ("dn", 3 * W), ("ab", 2 * H),
                  ("z1", W), ("dil", 3 * GROUPS * W), ("z2", W), ("gate", BRANCHES * D)):
    COL[_name] = _at
    _at += _n
IN_WIDTH = _at
A, B, C = 0, 1, 2
TWO_PI = 2.0 * np.pi
TWO_PI_PARTS = [6.28125]
TWO_PI_PARTS.append(float((np.float32(TWO_PI - 6.28125).view(np.uint32) & np.uint32(0xFFFFE000)).view(np.float32)))
TWO_PI_PARTS.append(float(np.float32(TWO_PI - sum(TWO_PI_PARTS))))
PI_BELOW = float(np.nextafter(np.float32(np.pi), np.float32(0)))
ROUND = 1.5 * 2.0 ** 23


def unit_list():
    def halves(what, i, n):
        return [(what, i, hf, KC // 2, n) for hf in range(2)]

    def merge(n):
        u = halves("z", n, W)
        for c in range(2):
            u += halves("gate", 2 * n + c, 512) + [("branch", 2 * n + c, 0, W // P, 512)]
        return u

    us = halves("latq", 0, Q_RANK + 2 * H) + halves("latkv", 0, KV_RANK + ROPE) + halves("dn", 0, W)
    us += [("qb", j, 0, Q_RANK // P, 2 * QK) for j in range(2)] + [("kvb", j, 0, KV_RANK // P, 4 * HD) for j in range(2)]
    us += halves("dn", 1, W) + halves("dn", 2, W) + merge(A)
    for g in range(GROUPS):
        for i in range(3):
            us += halves("dil", 3 * g + i, W)
    us += merge(C) + merge(B) + halves("out", 0, 512) + halves("out", 1, 512)
    return us


UNITS = unit_list()
NU = len(UNITS)
RAW, SPLIT = 3, 2
assert NU % RAW == 0 and NU % SPLIT == 0


def step_table():
    st = {u: [] for u in range(-1, NU)}

    def put(u, *steps):
        st[u] += steps

    put(-1, ("load",), ("norm",), *[("xT", k) for k in range(4)], ("m_tables",))
    put(1, ("dn_g0",), ("dn_g1",))
    put(2, ("dn_gc",))
    put(3, ("lat_norm",))
    put(4, ("latT", 0), ("latT", 1), ("latT", 2))
    put(5, ("dn_fT", 0, 0), ("dn_fT", 0, 1), ("dn_silu", 0), ("dn_sq", 0), ("kpe",))
    put(6, ("dn_ss", 0))
    put(7, ("q_norm",), ("dn_bT", 0, 0), ("dn_bT", 0, 1), ("q_rs",))
    put(8, ("tr", "q", 0), ("tr", "q", 1), ("q_rope", 0), ("q_rope", 1))
    put(9, ("tr", "qg", 0), ("tr", "qg", 1), ("k_norm",), ("tr", "mqn", 0), ("tr", "mqn", 1), ("k_rs",))
    put(10, ("tr", "mqp", 0), ("tr", "mqp", 1), ("tr", "mkn", 0), ("tr", "mkn", 1), ("tr", "mkp", 0))
    put(11, ("dn_fT", 1, 0), ("dn_fT", 1, 1), ("dn_silu", 1), ("dn_sq", 1), *scores("m", 0))
    put(12, *scores("m", 1), ("dn_ss", 1))
    put(13, ("pT", "m", 0, 0), ("dn_bT", 1, 0), ("dn_bT", 1, 1), ("dn_fT", 2, 0), ("dn_fT", 2, 1), ("dn_silu", 2))
    put(14, ("pv", "m", 0, 0), ("pT", "m", 1, 0), ("tr", "k", 0), ("tr", "k", 1), ("dn_row", 0), ("dn_row", 1))
    put(15, ("pv", "m", 1, 0), ("pT", "m", 1, 1), ("dn_bT", 2, 0), ("dn_bT", 2, 1))
    put(16, ("pv", "m", 1, 1), ("m_out",), ("dn_kk", 0), ("dn_kk", 1))
    put(17, ("yT", A, 0), ("yT", A, 1), ("dn_qk", 0), ("dn_qk", 1))
    put(19, ("dn_U", 0), ("dn_U", 1), ("dn_M", 1, 0), ("dn_M", 1, 1))
    put(21, ("d_tables",))
    u = 22
    for s in range(1, len(LEVELS)):
        put(u, ("dn_X", s, 0), ("dn_X", s, 1))
        put(u + 1, ("dn_TX", s, 0), ("dn_TX", s, 1))
        if s < len(LEVELS) - 1:
            put(u + 1, ("dn_M", s + 1, 0), ("dn_M", s + 1, 1))
        u += 2
    put(32, ("dn_u", 0), ("dn_u", 1), ("dn_v0",))
    put(33, ("dn_w", 0), ("dn_w", 1))
    put(34, ("dn_ds", 0))
    put(35, ("dn_ws", 1), ("dn_dec", 1))
    put(36, ("dn_ds", 1))
    put(37, ("dn_ws", 2), ("dn_dec", 2))
    put(38, ("dn_ds", 2))
    put(39, ("dn_ws", 3))
    for g in range(GROUPS):
        b = 23 + 6 * g
        put(b, ("d_sq", g, 0), ("d_rs", g, 0), ("d_rope", g, 0))
        put(b + 1, ("tr", "dq", 2 * g), ("tr", "dq", 2 * g + 1))
        put(b + 2, ("d_sq", g, 1), ("d_rs", g, 1), ("d_rope", g, 1))
        put(b + 3, ("tr", "dk", 2 * g), ("tr", "dk", 2 * g + 1))
        put(b + 4, *scores(g, 0), *scores(g, 1))
        put(b + 5, ("pT", g, 0, 0))
        put(b + 6, ("pv", g, 0, 0), ("pT", g, 1, 0))
        put(b + 7, ("pv", g, 1, 0), ("pT", g, 1, 1))
        put(b + 8, ("pv", g, 1, 1))
    put(41, ("d_c0",), ("d_c1",))
    put(42, ("d_out",))
    put(43, ("yT", C, 0), ("yT", C, 1))
    put(45, ("dn_o", 0), ("dn_o", 1), ("dn_on",))
    put(49, ("b_out",))
    put(50, ("yT", B, 0), ("yT", B, 1))
    put(55, *[("mT", k) for k in range(4)])
    return st


def scores(a, t):
    return [("sc", a, t, j) for j in range(t + 1)] + [("soft", a, t)]


def whole(u):
    return UNITS[u][0] in ("qb", "kvb", "branch")


def evict_step(u):
    what, i = UNITS[u][:2]
    return ({"z": "evict_z", "branch": "evict_branch" if i // 2 != A else "evict_first"}.get(what, "evict"), u)


STEPS = step_table()
ORDER = [("prep", 0), *STEPS[-1]]
for _u in range(NU):
    ORDER.append(("unit", _u))
    if _u + 1 < NU:
        ORDER.append(("prep", _u + 1))
    if whole(_u) or UNITS[_u][2] == 1:
        ORDER.append(evict_step(_u))
    ORDER += STEPS[_u]


def banks(step):
    k, *a = step
    if k == "unit":
        what, _, hf, _, _ = UNITS[a[0]]
        return [0, 1] if hf == 0 else []
    if k in ("xT", "mT"):
        return [4 + a[0]]
    if k == "latT":
        return [5 + a[0]]
    if k == "yT":
        return [4 + a[1] * 3]
    if k == "tr":
        return [{"q": 2, "qg": 2, "k": 2, "mqn": 5, "mqp": 5, "mkn": 5, "mkp": 7, "dq": 5, "dk": 5}[a[0]] + a[1] % 2]
    if k == "sc":
        return [5 + (a[2] if a[1] else 0)]
    if k == "pT":
        return [7]
    if k == "pv":
        return [4] if a[2] == 0 else []
    if k in ("dn_fT", "dn_bT"):
        return [2 + a[1]]
    if k in ("dn_gc", "dn_ss"):
        return [3]
    if k in ("dn_row", "dn_kk", "dn_qk", "dn_U", "dn_u", "dn_w", "dn_o"):
        return [2 + a[0]]
    if k == "dn_X":
        return [2 + a[1]]
    if k == "dn_TX":
        return [2, 3] if a[0] < len(LEVELS) - 1 else [2 + a[1]]
    if k == "dn_ws":
        return [2]
    if k == "dn_ds":
        return [3]
    return []


TURN, TURNS = {}, [0] * 8
for _s in ORDER:
    for _b in banks(_s):
        TURN[(_s, _b)] = TURNS[_b]
        TURNS[_b] += 1

RAW_AT, RAW_TOTAL = [], [0] * RAW
for _u in range(NU):
    RAW_TOTAL[_u % RAW] += 2 if UNITS[_u][0] == "latq" else 1
    RAW_AT.append(RAW_TOTAL[_u % RAW])

COUNT, PLACE = {}, {}
for _s in ORDER:
    PLACE[_s] = COUNT.get(_s[0], 0)
    COUNT[_s[0]] = PLACE[_s] + 1
HALVES = sum(u[2] == 0 and u[0] not in ("qb", "kvb", "branch") for u in UNITS)
GATES = [u[1] for u in UNITS if u[0] == "gate" and u[2] == 0]
OWN = {"vector": 48, "scalar": 1, "gpsimd": 49}

TAB, _at = {}, 0
for _name, _n in (("ident", P), ("tri", P), ("same", P), ("strict", P), ("level", P), *[(f"levelT{s}", P) for s in LEVELS],
                  *[(f"mask_{a}", 2 * P) for a in ("m", 0, 1, 2)], ("chunk", 2), ("one", 1), ("inv", ROPE // 2 + HD // 2),
                  ("inv_n", GROUPS), ("inv_d", 1), ("inv_hd", 1), ("inv_rope", 1), ("eps", 1), ("half", 1), ("q_scale", 1),
                  ("power", 1)):
    TAB[_name] = (_at, _n)
    _at += _n
TAB_COLS = _at
GAIN, _at = {}, 0
for _name, _n in (("mq", QK), ("mk", QK), ("dq", HD), ("dk", HD), ("dn", HD), ("a_log", H), ("dt", H)):
    GAIN[_name] = (_at, _n)
    _at += _n
GAIN_COLS = _at
ROWS_CONV, ROWS_NORM = CONV * 3 * H, KC
PRM_NORM, PRM_LAT = ROWS_CONV, ROWS_CONV + ROWS_NORM
PRM_ROWS = PRM_LAT + Q_RANK // P + KV_RANK // P


def shape_tables():
    i, j = np.arange(P)[:, None], np.arange(P)[None, :]
    same = i // CH == j // CH
    t = np.zeros((P, TAB_COLS), np.float32)

    def put(name, v):
        a, n = TAB[name]
        t[:, a:a + n] = v

    put("ident", i == j)
    put("tri", same & (i <= j))
    put("same", same)
    put("strict", same & (j < i))

    def level(s, r, c):
        return (r // (2 * s) == c // (2 * s)) & (r // s % 2 == 1) & (c // s % 2 == 0)

    put("level", level(1, i, j))
    for s in LEVELS:
        put(f"levelT{s}", level(s, j, i))
    for a, dil, prev in (("m", 1, i == i), (0, DILATIONS[0], j >= i), (1, DILATIONS[1], i == i), (2, DILATIONS[2], i == i)):
        ok = np.concatenate([prev & ((P + i - j) % dil == 0), (j <= i) & ((i - j) % dil == 0)], axis=1)
        put(f"mask_{a}", np.where(ok, 0.0, NEG))
    put("chunk", np.arange(P)[:, None] // CH == np.arange(2)[None, :])
    put("one", 1.0)
    theta = np.float32(10000.0)
    put("inv", np.concatenate([np.float32(1.0) / theta ** (np.arange(0, n, 2, dtype=np.float32) / np.float32(n)) for n in (ROPE, HD)])[None])
    put("inv_n", np.array([1.0 / Q_RANK, 1.0 / KV_RANK, 1.0 / ROPE], np.float32)[None])
    for name, v in (("inv_d", 1.0 / D), ("inv_hd", 1.0 / HD), ("inv_rope", 1.0 / ROPE), ("eps", EPS), ("half", 0.5),
                    ("q_scale", HD ** -0.5), ("power", -0.5)):
        put(name, v)
    return t


def hybrid_trunk(nc, x, positions, norm_g, w_in, mla_q_a_norm_g, mla_w_q_b, mla_kv_a_norm_g, mla_w_kv_b,
                 mla_q_norm_g, mla_k_norm_g, dn_conv_w, dn_a_log, dn_dt_bias, dn_out_norm_g,
                 dil_q_norm_g, dil_k_norm_g, w_branch, w_out, tables, out):
    with ExitStack() as ctx:
        def sb(name, cols, dt=F32, rows=P):
            return ctx.enter_context(nc.sbuf_tensor(name, [rows, cols], dt))

        def sem(name):
            return ctx.enter_context(nc.semaphore(name))

        def v3(ap, a):
            return ap.rearrange("p (a b) -> p a b", a=a)

        tab = sb("tab", TAB_COLS)
        xs = v3(sb("xs", NT * D)[:, :], NT)
        gain = sb("gain", GAIN_COLS)
        prm_all = sb("prm_all", DEPTH * PRM_ROWS)
        prm = sb("prm", PRM_ROWS)
        rot = {n: [v3(sb(f"rot{n}{i}", NT * n)[:, :], NT) for i in range(2)] for n in (ROPE, HD)}
        raw = sb("raw", RAW * 2048)
        w_hi, w_lo = sb("w_hi", SPLIT * 2048, F32R), sb("w_lo", SPLIT * 2048, F32R)
        hT = [v3(sb(f"hT{i}", KC * S, F32R)[:, :], KC) for i in range(2)]
        yT = [v3(sb(f"yT{i}", 5 * S, F32R)[:, :], 5) for i in range(2)]
        gate = v3(sb("gate", NT * 512)[:, :], NT)
        mixed = v3(sb("mixed", NT * D)[:, :], NT)
        z = v3(sb("z", NT * W)[:, :], NT)
        dn = sb("dn", 10 * NT * W)
        at = sb("at", 10880)
        prm_rows = at[0:PRM_ROWS, 0:DEPTH * P]
        sm = sb("sm", 640)

        def dnbuf(i):
            return v3(dn[:, i * NT * W:(i + 1) * NT * W], NT)

        def heads(ap):
            return ap.rearrange("p (h d) -> p h d", h=H)

        mix = d_D = dnbuf(0)
        conv = d_U = dnbuf(1)
        th = d_Dt = dnbuf(2)
        d_T = dnbuf(3)
        kn = dnbuf(3)
        qT = d_TT = dnbuf(4)
        kT = d_Us = dnbuf(5)
        qgT = dnbuf(6)
        qg = kbg = dnbuf(7)
        qn = kdec = dnbuf(8)
        vb = dnbuf(9)
        L, Aqk, X = d_D, d_Dt, d_D
        u_, wT, vnew = d_T, d_U, X
        states = [None] + [dn[:, (4 + i // 2) * NT * W + (i % 2) * W:(4 + i // 2) * NT * W + (i % 2 + 1) * W] for i in range(3)]
        o_sb = kbg
        o_sq = vb
        feat = conv.rearrange("p t n -> p (t n)").rearrange("p (f s) -> p f s", f=H)
        th_f = th.rearrange("p t n -> p (t n)").rearrange("p (f s) -> p f s", f=H)

        off = [0]

        def atb(cols, back=None):
            a = off[0] if back is None else back
            off[0] = a + cols
            return at[:, a:a + cols]

        Sc = [v3(atb((t + 1) * H * P), H) for t in range(NT)]
        PT = v3(atb(1024), 2)
        base = off[0]
        lat = v3(atb(NT * (Q_RANK + KV_RANK + ROPE)), NT)
        mq = v3(atb(NT * H * QK), NT)
        kv = v3(atb(NT * H * 2 * HD), NT)
        mqnT, mqpT, mknT = (v3(atb(1024), H) for _ in range(3))
        mkpT = atb(S)
        assert off[0] <= 10880, off
        off[0] = base
        stg = v3(atb(1024), NT)
        dqT, dkT = (v3(atb(1024), H) for _ in range(2))
        dv = v3(atb(1024), NT)
        rg = {k: [v3(atb(NT * HD), NT) for _ in range(2)] for k in ("dq", "dk")}
        og = [v3(atb(1024), NT) for _ in range(GROUPS)]
        assert off[0] <= 10880, off
        spare = mixed[:, 1, D - 4 * NT * ROPE:]
        rg.update({k: [v3(spare[:, (2 * n + i) * NT * ROPE:(2 * n + i + 1) * NT * ROPE], NT) for i in range(2)]
                   for n, k in enumerate(("mq", "mk"))})

        m_o = [mq.rearrange("p t n -> p (t n)")[:, t * W:(t + 1) * W] for t in range(NT)]

        so = [0]

        def small(n):
            so[0] += n
            assert so[0] <= 640
            return sm[:, so[0] - n:so[0]]

        ss_x, rstd, hrstd, rtmp = (small(NT) for _ in range(4))
        lss = v3(small(NT * 3), NT)
        lrs = v3(small(NT * 3), NT)
        ab = v3(small(NT * 2 * H), NT)
        a1, na, rl, lnp, g_, bt, beta, egc, edec, gdiff, begc = (v3(small(NT * H), NT) for _ in range(11))
        ea = small(H)
        gcs = v3(small(NT * 16), NT)
        eS = v3(small(NT * 2 * H), NT)
        ssd = [v3(small(NT * H), NT) for _ in range(2)]
        rq, rqg, rk, rkbg, rkd = (v3(small(NT * H), NT) for _ in range(5))
        oss = v3(small(NT * H), NT)
        ors = v3(small(NT * H), NT)
        hss = v3(small(NT * 12), NT)
        hrs = v3(small(NT * 12), NT)
        dss = v3(small(NT * H), NT)
        drs = v3(small(NT * H), NT)
        mx, nmx, den = (small(4 * NT * H).rearrange("p (a t h) -> p a t h", a=4, t=NT) for _ in range(3))
        mr = v3(small(NT * H), NT)
        csum = v3(small(NT * H), NT)
        cmax = v3(small(NT * H), NT)
        cexp = small(GROUPS * NT * H).rearrange("p (a t h) -> p a t h", a=GROUPS, t=NT)
        cden = small(GROUPS * NT * H).rearrange("p (a t h) -> p a t h", a=GROUPS, t=NT)
        pos_i = small(NT).bitcast(I32)
        pos_f = small(NT)

        def const(name):
            a, n = TAB[name]
            return tab[:, a:a + n]

        def gains(name):
            a, n = GAIN[name]
            return gain[:, a:a + n]

        def scale_of(a):
            return (QK if a == "m" else HD) ** -0.5

        ident = const("ident")

        def over_heads(ap):
            return ap.unsqueeze(1).broadcast_to([P, H, ap.shape[-1]])

        def per_head(ap, n=HD, h=H):
            return ap.unsqueeze(2).broadcast_to([P, h, n])

        ps = [ctx.enter_context(nc.psum_tensor(f"bank{b}", [P, 512], F32)) for b in range(8)]

        bank_full = [sem(f"bank_full{b}") for b in range(8)]
        bank_free = [sem(f"bank_free{b}") for b in range(8)]
        raw_loaded = [sem(f"raw_loaded{s}") for s in range(RAW)]
        start = {k: sem(k) for k in ("tab_loaded", "x_loaded", "pos_loaded", "rows_loaded", "rows_T", "rows_copied",
                                     "angle_step", "angles", "sines", "rot_ready", "stored")}
        gains_loaded, hi_done, lo_done, half_done = (sem(k) for k in ("gains_loaded", "hi_done", "lo_done", "half_done"))
        own = {e: sem(f"{e}_own") for e in OWN}
        seen = dict.fromkeys(OWN, 0)
        part_done = {}

        OPEN = 1

        def full(step, layer, i=0):
            b = banks(step)[i]
            return bank_full[b], layer * TURNS[b] + OPEN + TURN[(step, b)] + 1

        def free(step, layer, i=0):
            b = banks(step)[i]
            return bank_free[b], layer * TURNS[b] + OPEN + TURN[(step, b)]

        def taken(step, layer, i=0):
            b = banks(step)[i]
            return bank_free[b], layer * TURNS[b] + OPEN + TURN[(step, b)] + 1

        def part(engine, step):
            key = f"{engine}_{step[0]}"
            if key not in part_done:
                part_done[key] = sem(key)
            return part_done[key]

        def after(engine, step, layer):
            return part(engine, step), layer * COUNT[step[0]] + PLACE[step] + 1

        def bank_unit(u):
            return ("unit", u - UNITS[u][2])

        def used(u, layer):
            if banks(("unit", u)) and not whole(u):
                return half_done, layer * HALVES + sum(bool(banks(("unit", v))) and not whole(v) for v in range(u)) + 1
            return full(bank_unit(u), layer, 1)

        def block_taken(u, layer):
            return taken(bank_unit(u), layer, 1)

        LAST = NU - 1

        def layer_start(layer):
            return bank_free[1], layer * TURNS[1] + OPEN

        def unit_of(what, i):
            return max(u for u in range(NU) if UNITS[u][:2] == (what, i))

        def view(buf, slot, nk, n):
            return buf[:, slot * 2048:slot * 2048 + nk * n].rearrange("p (c n) -> p c n", c=nk)

        def piece(nk, i):
            cut = (nk + 1) // 2
            return (0, cut) if i == 0 else (cut, nk)

        x_rows = x.rearrange("b (t p) d -> (b p) t d", p=P)
        out_rows = out.rearrange("b (t p) d -> (b p) t d", p=P)
        win = w_in.rearrange("l (c p) n -> l p c n", p=P)
        wqb = mla_w_q_b.rearrange("l (c p) n -> l p c n", p=P)
        wkvb = mla_w_kv_b.rearrange("l (c p) n -> l p c n", p=P)
        wbr = w_branch.rearrange("l b (c p) n -> l b p c n", p=P)
        wout = w_out.rearrange("l (c p) n -> l p c n", p=P)

        def sources(u, layer):
            what, i, hf, nk, n = UNITS[u]
            rows = slice(hf * nk, (hf + 1) * nk)
            if what == "qb":
                return [(0, wqb[layer, :, :, i * n:(i + 1) * n])]
            if what == "kvb":
                return [(0, wkvb[layer, :, :, i * n:(i + 1) * n])]
            if what == "branch":
                return [(0, wbr[layer, i // 2, :, :, (i % 2) * n:(i % 2 + 1) * n])]
            if what == "out":
                return [(0, wout[layer, :, rows, i * n:(i + 1) * n])]
            if what == "latq":
                return [(0, win[layer, :, rows, COL["ab"]:COL["ab"] + 2 * H]),
                        (2 * H, win[layer, :, rows, COL["q_lat"]:COL["q_lat"] + Q_RANK])]
            c = {"latkv": lambda: COL["kv_lat"], "dn": lambda: COL["dn"] + i * W, "z": lambda: COL[f"z{i}"],
                 "gate": lambda: COL["gate"] + i * 512,
                 "dil": lambda: COL["dil"] + (i % 3) * GROUPS * W + (i // 3) * W}[what]()
            return [(0, win[layer, :, rows, c:c + n])]

        block = ctx.enter_context(nc.Block())

        @block.sync
        def _(sp):
            for s in (*bank_free, *bank_full, lo_done):
                sp.sem_inc(s, OPEN)
            sp.dma_start(xs, x_rows).then_inc(start["x_loaded"], 16)
            sp.dma_start(tab[:, 0:P], tables[:, 0:P]).then_inc(start["tab_loaded"], 16)
            for r0, src in ((0, dn_conv_w.rearrange("l j (f p) -> (j f) l p", p=P)), (PRM_NORM, norm_g.rearrange("l (c p) -> c l p", p=P)),
                            (PRM_LAT, mla_q_a_norm_g.rearrange("l (c p) -> c l p", p=P)),
                            (PRM_LAT + Q_RANK // P, mla_kv_a_norm_g.rearrange("l (c p) -> c l p", p=P))):
                sp.dma_start(v3(prm_rows[r0:r0 + src.shape[0], :], DEPTH), src).then_inc(start["rows_loaded"], 16)
            with sp.Fori(0, DEPTH) as layer:
                for u in range(NU):
                    what, i, hf, nk, n = UNITS[u]
                    if u < RAW:
                        sp.wait_ge(lo_done, layer * (PIECES * NU) + OPEN)
                    else:
                        sp.wait_ge(lo_done, layer * (PIECES * NU) + OPEN + PIECES * (u - RAW + 1))
                    dst = view(raw, u % RAW, nk, n)
                    for c, src in sources(u, layer):
                        sp.dma_start(dst[:, :, c:c + src.shape[-1]], src).then_inc(raw_loaded[u % RAW], 16)
                    if u == RAW - 1:
                        sp.wait_ge(*layer_start(layer))
                        for name, src in (("mq", mla_q_norm_g), ("mk", mla_k_norm_g), ("dq", dil_q_norm_g), ("dk", dil_k_norm_g),
                                          ("dn", dn_out_norm_g), ("a_log", dn_a_log), ("dt", dn_dt_bias)):
                            v = src[layer]
                            sp.dma_start(gains(name), v.unsqueeze(0).broadcast_to([P, v.shape[0]])).then_inc(gains_loaded, 16)
            sp.wait_ge(bank_free[1], DEPTH * TURNS[1] + OPEN)
            sp.dma_start(out_rows, xs).then_inc(start["stored"], 16)
            sp.wait_ge(start["stored"], 16)

        @block.tensor
        def _(pe):
            mm, tr = nc.tensor.matmul, nc.tensor.transpose

            def unit(step, layer):
                u = step[1]
                what, i, hf, nk, n = UNITS[u]
                hi, lo = view(w_hi, u % SPLIT, nk, n), view(w_lo, u % SPLIT, nk, n)
                starts, ends = whole(u) or hf == 0, whole(u) or hf == 1
                src, k0 = (yT, 3 if what == "kvb" else 0) if whole(u) else (hT, hf * nk)
                if u == 0:
                    pe.wait_ge(*taken(("xT", 3), layer))
                if what == "qb":
                    pe.wait_ge(*taken(("latT", 2), layer))
                if what == "branch":
                    pe.wait_ge(*taken(("yT", i // 2, 1), layer))
                if what == "out":
                    pe.wait_ge(*taken(("mT", 3), layer))
                for t in range(NT):
                    if starts:
                        pe.wait_ge(*free(step, layer, t))
                    tok = slice(t * P, (t + 1) * P)
                    o = ps[t][:, 0:n]
                    for k in range(nk):
                        if t == 0 and k in (0, piece(nk, 1)[0]):
                            pe.wait_ge(lo_done, layer * (PIECES * NU) + OPEN + PIECES * u + 1 + (k > 0))
                        mm(o, src[0][:, k0 + k, tok], hi[:, k, :], start=starts and k == 0, stop=False)
                        mm(o, src[0][:, k0 + k, tok], lo[:, k, :], start=False, stop=False)
                        last = mm(o, src[1][:, k0 + k, tok], hi[:, k, :], start=False, stop=ends and k == nk - 1)
                    if ends:
                        last.then_inc(bank_full[t], 1)
                if not ends:
                    last.then_inc(half_done, 1)

            def four(step, layer, product, i=0):
                pe.wait_ge(*free(step, layer, i))
                b = banks(step)[i]
                for h in range(H):
                    last = product(ps[b][:, h * P:(h + 1) * P], h)
                last.then_inc(bank_full[b], 1)

            def wait_taken(step, layer, *made):
                latest = {}
                for s in made:
                    s, i = s if isinstance(s[0], tuple) else (s, 0)
                    b = banks(s)[i]
                    latest[b] = max(latest.get(b, 0), TURN[(s, b)] + 1)
                for b, k in latest.items():
                    if b not in banks(step)[:1]:
                        pe.wait_ge(bank_free[b], layer * TURNS[b] + OPEN + k)

            def square(src, jp):
                return lambda o, j: tr(o, src[:, j % 2, (2 * jp + j // 2) * P:(2 * jp + j // 2 + 1) * P], ident)

            def hd(buf, t, h):
                return buf[:, t, h * P:(h + 1) * P]

            def xT(step, layer):
                if step[1] == 0:
                    pe.wait_ge(*layer_start(layer))
                four(step, layer, square(xs, step[1]))

            def mT(step, layer):
                if step[1] == 0:
                    pe.wait_ge(*after("gpsimd", evict_step(unit_of("branch", GATES[-1])), layer))
                four(step, layer, square(mixed, step[1]))

            def yT_step(step, layer):
                _, n, jp = step
                pe.wait_ge(*after("vector", {A: ("m_out",), B: ("b_out",), C: ("d_out",)}[n], layer))
                four(step, layer, square(z, jp))

            def latT(step, layer):
                j = step[1]
                pe.wait_ge(*block_taken(3, layer))
                pe.wait_ge(*free(step, layer))
                b = banks(step)[0]
                for c in range(2 * j, min(2 * j + 2, 5)):
                    for t in range(NT):
                        last = tr(ps[b][:, (c % 2) * S + t * P:(c % 2) * S + (t + 1) * P], lat[:, t, c * P:(c + 1) * P], ident)
                last.then_inc(bank_full[b], 1)

            def tr_step(step, layer):
                _, what, i = step
                t = i % 2
                if what == "mkp":
                    pe.wait_ge(*after("gpsimd", ("kpe",), layer))
                    pe.wait_ge(*free(step, layer))
                    for tt in range(NT):
                        last = tr(ps[7][:, tt * P:(tt + 1) * P], lat[:, tt, Q_RANK + KV_RANK + ROPE - P:], ident)
                    last.then_inc(bank_full[7], 1)
                    return
                if what in ("q", "qg", "k"):
                    wait_taken(step, layer, ("dn_bT", int(what == "k"), t))
                else:
                    pe.wait_ge(*{
                             "mqn": lambda: after("vector", ("q_rope", t), layer), "mqp": lambda: after("gpsimd", ("q_rope", t), layer),
                             "mkn": lambda: after("vector", ("k_rs",), layer),
                             "dq": lambda: after("gpsimd", ("d_rope", i // 2, 0), layer),
                             "dk": lambda: after("gpsimd", ("d_rope", i // 2, 1), layer)}[what]())
                src = {"q": lambda h: hd(qn, t, h), "qg": lambda h: hd(qg, t, h), "k": lambda h: hd(kn, t, h),
                       "mqn": lambda h: mq[:, t, h * QK:h * QK + HD], "mqp": lambda h: mq[:, t, (h + 1) * QK - P:(h + 1) * QK],
                       "mkn": lambda h: kv[:, t, h * 2 * HD:h * 2 * HD + HD],
                       "dq": lambda h: hd(gate, t, h), "dk": lambda h: hd(gate, t, h)}[what]
                four(step, layer, lambda o, h: tr(o, src(h), ident))

            def sc(step, layer):
                _, a, t, j = step
                nk = (t + 1) * P
                if t == 0:
                    wait_taken(step, layer, *((("tr", "mkn", 1), ("tr", "mkp", 0)) if a == "m" else (("tr", "dk", 2 * a + 1),)))
                pe.wait_ge(*free(step, layer))
                b = banks(step)[0]
                tok = slice(t * P, (t + 1) * P)
                for n, h in enumerate(range(H) if t == 0 else (2 * j, 2 * j + 1)):
                    o = ps[b][:, n * nk:(n + 1) * nk]
                    if a == "m":
                        mm(o, mqnT[:, h, tok], mknT[:, h, 0:nk], start=True, stop=False)
                        last = mm(o, mqpT[P - ROPE:, h, tok], mkpT[P - ROPE:, 0:nk], start=False, stop=True)
                    else:
                        last = mm(o, dqT[:, h, tok], dkT[:, h, 0:nk], start=True, stop=True)
                last.then_inc(bank_full[b], 1)

            def pT(step, layer):
                _, a, t, j = step
                pe.wait_ge(*after("scalar", ("soft", a, t), layer))

                def one(o, n):
                    h, k = (n, 0) if t == 0 else (2 * j + n // 2, n % 2)
                    return tr(o, Sc[t][:, h, k * P:(k + 1) * P], ident)

                four(step, layer, one)

            def pv(step, layer):
                _, a, t, j = step
                pe.wait_ge(*taken(("pT", a, t, j), layer))
                pe.wait_ge(*block_taken(unit_of("kvb", 1) if a == "m" else unit_of("dil", 3 * a + 2), layer))
                if j == 0:
                    pe.wait_ge(*free(step, layer))
                pt = PT[:, PLACE[("pT", a, t, j)] % 2, :]

                def value(h, kt):
                    return kv[:, kt, h * 2 * HD + HD:(h + 1) * 2 * HD] if a == "m" else hd(dv, kt, h)

                for h in (range(H) if t == 0 else (2 * j, 2 * j + 1)):
                    for kt in range(t + 1):
                        c = (h if t == 0 else h % 2 * 2 + kt) * P
                        last = mm(ps[4][:, h * P:(h + 1) * P], pt[:, c:c + P], value(h, kt), start=kt == 0, stop=kt == t)
                if j == t:
                    last.then_inc(bank_full[4], 1)

            def dn_gc(step, layer):
                pe.wait_ge(*after("vector", ("dn_g1",), layer))
                pe.wait_ge(*free(step, layer))
                for t in range(NT):
                    for i, w in enumerate((const("tri"), const("same"), const("chunk")[:, 0:1].broadcast_to([P, P]),
                                           const("chunk")[:, 1:2].broadcast_to([P, P]))):
                        last = mm(ps[3][:, (t * 4 + i) * H:(t * 4 + i + 1) * H], w, g_[:, t, :], start=True, stop=True)
                last.then_inc(bank_full[3], 1)

            def dn_row(step, layer):
                t = step[1]
                four(step, layer, lambda o, h: mm(o, g_[:, t, h:h + 1].broadcast_to([P, P]), const("tri"), start=True, stop=True))

            def dn_fT(step, layer):
                _, i, j = step
                pe.wait_ge(*block_taken(unit_of("dn", i), layer))
                four(step, layer, square(mix, j))

            def dn_ss(step, layer):
                pe.wait_ge(*after("gpsimd", ("dn_sq", step[1]), layer))
                pe.wait_ge(*free(step, layer))
                for t in range(NT):
                    for h in range(H):
                        last = mm(ps[3][:, t * H + h:t * H + h + 1], th_f[:, h, t * P:(t + 1) * P], const("one"), start=True, stop=True)
                last.then_inc(bank_full[3], 1)

            def dn_bT(step, layer):
                _, i, t = step
                pe.wait_ge(*after("vector", ("dn_silu", i), layer))
                four(step, layer, lambda o, h: tr(o, feat[:, h, t * P:(t + 1) * P], ident))

            def dn_kk(step, layer):
                t = step[1]
                wait_taken(step, layer, ("tr", "k", t))
                four(step, layer, lambda o, h: mm(o, hd(kT, t, h), hd(kT, t, h), start=True, stop=True))

            def dn_qk(step, layer):
                t = step[1]
                wait_taken(step, layer, ("tr", "q", t))
                four(step, layer, lambda o, h: mm(o, hd(kT, t, h), hd(qT, t, h), start=True, stop=True))

            def dn_U(step, layer):
                t = step[1]
                wait_taken(step, layer, ("dn_kk", t))
                four(step, layer, lambda o, h: tr(o, hd(L, t, h), ident))

            def dn_X(step, layer):
                _, s, t = step
                pe.wait_ge(*after("gpsimd", ("dn_M", s, t), layer))
                if s == 1:
                    pe.wait_ge(*after("gpsimd", ("dn_U", t), layer))
                else:
                    wait_taken(step, layer, (("dn_TX", s - 1, t), 0))
                four(step, layer, lambda o, h: mm(o, hd(d_Us, t, h), hd(d_T, t, h), start=True, stop=True))

            def dn_TX(step, layer):
                _, s, t = step
                wait_taken(step, layer, ("dn_X", s, t), *([(("dn_TX", s - 1, t), 1)] if s > 1 else []))
                final = s == len(LEVELS) - 1
                if not final:
                    four(step, layer, lambda o, h: mm(o, hd(d_TT, t, h), hd(X, t, h), start=True, stop=True), 0)
                four(step, layer, lambda o, h: mm(o, hd(X, t, h), hd(d_TT, t, h), start=True, stop=True), 0 if final else 1)

            def dn_u(step, layer):
                t = step[1]
                wait_taken(step, layer, ("dn_TX", len(LEVELS) - 1, t), ("dn_bT", 2, t))
                four(step, layer, lambda o, h: mm(o, hd(d_TT, t, h), hd(vb, t, h), start=True, stop=True))

            def dn_w(step, layer):
                t = step[1]
                four(step, layer, lambda o, h: mm(o, hd(kbg, t, h), hd(d_TT, t, h), start=True, stop=True))

            def dn_ds(step, layer):
                c = step[1]
                t, r = c // 2, slice(CH * (c % 2), CH * (c % 2) + CH)
                if c == 0:
                    pe.wait_ge(*after("vector", ("dn_v0",), layer))
                else:
                    wait_taken(step, layer, ("dn_ws", c))
                four(step, layer, lambda o, h: mm(o, hd(kdec, t, h)[r, :], hd(vnew, t, h)[r, :], start=True, stop=True))

            def dn_ws(step, layer):
                c = step[1]
                t, r = c // 2, slice(CH * (c % 2), CH * (c % 2) + CH)
                wait_taken(step, layer, ("dn_w", t), ("dn_ds", c - 1))
                four(step, layer, lambda o, h: mm(o[r, :], hd(wT, t, h)[:, r], states[c][:, h * P:(h + 1) * P], start=True, stop=True))

            def dn_o(step, layer):
                t = step[1]
                wait_taken(step, layer, ("dn_ws", 2 * t + 1), ("tr", "qg", t), ("dn_qk", t))

                def one(o, h):
                    mm(o, hd(Aqk, t, h), hd(vnew, t, h), start=True, stop=False, skip_group_check=True)
                    for c in (2 * t, 2 * t + 1):
                        if c > 0:
                            r = slice(CH * (c % 2), CH * (c % 2) + CH)
                            last = mm(o[r, :], hd(qgT, t, h)[:, r], states[c][:, h * P:(h + 1) * P], start=False, stop=True,
                                      skip_group_check=True)
                    return last

                four(step, layer, one)

            parts = {"unit": unit, "xT": xT, "mT": mT, "yT": yT_step, "latT": latT, "tr": tr_step, "sc": sc, "pT": pT, "pv": pv,
                     "dn_gc": dn_gc, "dn_row": dn_row, "dn_fT": dn_fT, "dn_ss": dn_ss, "dn_bT": dn_bT, "dn_kk": dn_kk,
                     "dn_qk": dn_qk, "dn_U": dn_U, "dn_X": dn_X, "dn_TX": dn_TX, "dn_u": dn_u, "dn_w": dn_w, "dn_ds": dn_ds,
                     "dn_ws": dn_ws, "dn_o": dn_o}
            pe.wait_ge(start["tab_loaded"], 32)
            pe.wait_ge(start["rows_loaded"], 64)
            for d in range(DEPTH):
                last = tr(ps[7][:, d * PRM_ROWS:(d + 1) * PRM_ROWS], prm_rows[:, d * P:(d + 1) * P], ident[0:PRM_ROWS, 0:PRM_ROWS])
            last.then_inc(start["rows_T"], 1)
            pe.wait_ge(start["rows_copied"], 1)
            pe.wait_ge(start["x_loaded"], 16)
            with pe.Fori(0, DEPTH) as layer:
                for step in ORDER:
                    if step[0] in parts:
                        parts[step[0]](step, layer)

        @block.scalar
        def _(act):
            av = nc.scalar.activation

            def own_next(ins, layer):
                seen["scalar"] += 1
                ins.then_inc(own["scalar"], 1)
                act.wait_ge(own["scalar"], layer * OWN["scalar"] + seen["scalar"])

            def prep(step, layer):
                u = step[1]
                what, i, hf, nk, n = UNITS[u]
                act.wait_ge(raw_loaded[u % RAW], layer * (16 * RAW_TOTAL[u % RAW]) + 16 * RAW_AT[u])
                act.wait_ge(*(used(u - SPLIT, layer) if u >= SPLIT else (bank_full[1], layer * TURNS[1] + OPEN)))
                for p in range(PIECES):
                    a, b = piece(nk, p)
                    av(view(w_hi, u % SPLIT, nk, n)[:, a:b, :], view(raw, u % RAW, nk, n)[:, a:b, :], ACT.Copy).then_inc(hi_done, 1)

            def evict(step, layer):
                u = step[1]
                what, i, hf, nk, n = UNITS[u]
                key = bank_unit(u)
                if what == "out":
                    return
                if what == "latq":
                    act.wait_ge(*after("gpsimd", ("norm",), layer))
                elif what == "dn" and i > 0:
                    act.wait_ge(*full(("dn_fT", i - 1, 1), layer))
                elif what in ("qb", "kvb") and i == 0:
                    act.wait_ge(*after("gpsimd", ("lat_norm",), layer))
                elif what == "dil" and i % 3 < 2:
                    if i == 0:
                        act.wait_ge(*full(("pv", "m", 1, 0), layer))
                        act.wait_ge(*after("vector", ("m_out",), layer))
                    else:
                        act.wait_ge(*after("gpsimd", ("d_rope", (i - 1) // 3, 0) if i % 3 == 1 else ("d_rope", i // 3 - 1, 1), layer))
                elif what == "z" and i != A:
                    act.wait_ge(*full(("yT", {C: A, B: C}[i], 1), layer))
                elif what == "gate":
                    if i == GATES[0]:
                        for e in ("gpsimd", "vector"):
                            act.wait_ge(*after(e, ("q_rope", 1), layer))
                        act.wait_ge(*after("gpsimd", ("kpe",), layer))
                    else:
                        b = unit_of("branch", GATES[GATES.index(i) - 1])
                        act.wait_ge(*(block_taken(b, layer) if UNITS[b][1] // 2 == A else after("gpsimd", evict_step(b), layer)))
                    if i == 2 * C:
                        act.wait_ge(*full(("tr", "dk", 2 * GROUPS - 1), layer))
                for t in range(NT):
                    if what == "dil" and i % 3 == 2 and i > 2 and t == 0:
                        act.wait_ge(*full(("pv", i // 3 - 1, 1, 0), layer))
                    act.wait_ge(*full(key, layer, t))
                    o = ps[t][:, 0:n]
                    if what == "latq":
                        av(ab[:, t, :], o[:, 0:2 * H], ACT.Copy, scale=rstd[:, t:t + 1])
                        dst, o, func, scale = lat[:, t, 0:Q_RANK], o[:, 2 * H:n], ACT.Copy, rstd[:, t:t + 1]
                    elif what == "latkv":
                        dst, func, scale = lat[:, t, Q_RANK:], ACT.Copy, rstd[:, t:t + 1]
                    elif what == "dn":
                        dst, func, scale = mix[:, t, :], ACT.Copy, rstd[:, t:t + 1]
                    elif what == "qb":
                        dst, func, scale = mq[:, t, i * n:(i + 1) * n], ACT.Copy, lrs[:, t, 0:1]
                    elif what == "kvb":
                        dst, func, scale = kv[:, t, i * n:(i + 1) * n], ACT.Copy, lrs[:, t, 1:2]
                    elif what == "dil":
                        dst, func, scale = (stg if i % 3 < 2 else dv)[:, t, :], ACT.Copy, rstd[:, t:t + 1]
                    elif what == "z":
                        dst, func, scale = z[:, t, :], ACT.Tanh, hrstd[:, t:t + 1]
                    elif what == "gate":
                        dst, func, scale = gate[:, t, :], ACT.Tanh, hrstd[:, t:t + 1]
                    ins = av(dst, o, func, scale=scale)
                    if what != "z":
                        ins.then_inc(bank_free[t], 1)
                    elif t == 1:
                        ins.then_inc(part("scalar", step), 1)

            def norm(step, layer):
                act.wait_ge(start["x_loaded"], 16)
                act.wait_ge(start["rot_ready"], 1)
                act.wait_ge(*layer_start(layer))
                for t in range(NT):
                    last = av(mixed[:, t, :], xs[:, t, :], ACT.Square, accum_out=ss_x[:, t:t + 1])
                last.then_inc(part("scalar", step), 1)

            def split_hi(step, layer, k0, dst, scale, n=2):
                act.wait_ge(*full(step, layer))
                for j in range(n):
                    last = av(dst[0][:, k0 + j, :], ps[banks(step)[0]][:, j * S:(j + 1) * S], ACT.Copy, scale=scale(k0 + j))
                last.then_inc(part("scalar", step), 1)

            def xT(step, layer):
                act.wait_ge(*after("vector", ("load",), layer))
                split_hi(step, layer, 2 * step[1], hT, lambda c: prm[:, PRM_NORM + c:PRM_NORM + c + 1])

            def mT(step, layer):
                split_hi(step, layer, 2 * step[1], hT, lambda c: 0.5)

            def latT(step, layer):
                j = step[1]
                split_hi(step, layer, 2 * j, yT, lambda c: prm[:, PRM_LAT + c:PRM_LAT + c + 1], 2 if j < 2 else 1)

            def yT_step(step, layer):
                _, n, j = step
                act.wait_ge(*used({A: unit_of("kvb", 1), C: unit_of("branch", 2 * A + 1), B: unit_of("branch", 2 * C + 1)}[n], layer))
                split_hi(step, layer, 2 * j, yT, lambda c: 1.0)

            def lat_norm(step, layer):
                act.wait_ge(*block_taken(3, layer))
                junk = at[:, 0:NT * 704]
                for t in range(NT):
                    for i, (a, b) in enumerate(((0, Q_RANK), (Q_RANK, Q_RANK + KV_RANK), (Q_RANK + KV_RANK, 704))):
                        last = av(junk[:, t * 704 + a:t * 704 + b], lat[:, t, a:b], ACT.Square, accum_out=lss[:, t, i:i + 1])
                last.then_inc(part("scalar", step), 1)

            def dn_g0(step, layer):
                act.wait_ge(*after("vector", step, layer))
                av(ea, gains("a_log"), ACT.Exp)
                av(bt, ab[:, :, H:2 * H], ACT.Tanh, scale=0.5)
                own_next(av(na, na, ACT.Exp), layer)
                av(lnp, na, ACT.Ln, bias=1.0).then_inc(part("scalar", step), 1)

            def dn_gc(step, layer):
                act.wait_ge(*after("vector", step, layer))
                av(egc, gcs[:, :, 0:H], ACT.Exp)
                av(eS, gcs[:, :, 2 * H:4 * H], ACT.Exp)
                av(edec, gdiff, ACT.Exp).then_inc(part("scalar", step), 1)

            def dn_row(step, layer):
                t = step[1]
                act.wait_ge(*after("vector", step, layer))
                av(d_D[:, t, :], d_D[:, t, :], ACT.Exp, scale=-1.0)
                av(d_Dt[:, t, :], d_Dt[:, t, :], ACT.Exp).then_inc(part("scalar", step), 1)

            def dn_fT(step, layer):
                j = step[2]
                act.wait_ge(*taken(step, layer))
                av(th_f[:, 2 * j:2 * j + 2, :], feat[:, 2 * j:2 * j + 2, :], ACT.Tanh).then_inc(part("scalar", step), 1)

            def copies(step, layer):
                k, *a = step
                b = banks(step)[0]
                src = ps[b][:, :]
                t = a[-1] % 2
                tok = slice(t * P, (t + 1) * P)
                act.wait_ge(*full(step, layer))
                if k == "tr":
                    what = a[0]
                    if what == "mkp":
                        act.copy(mkpT[P - ROPE:, :], src[P - ROPE:, 0:S]).then_inc(bank_free[b], 1)
                        return
                    if what in ("q", "qg", "k"):
                        dst = {"q": qT, "qg": qgT, "k": kT}[what][:, t, :]
                    else:
                        r0 = P - ROPE if what == "mqp" else 0
                        dst = {"mqn": mqnT, "mqp": mqpT, "mkn": mknT, "dq": dqT, "dk": dkT}[what][r0:, :, tok]
                        src = heads(src[r0:, :])
                elif k == "pT":
                    dst = PT[:, PLACE[step] % 2, :]
                elif k == "pv":
                    if a[1] != a[2]:
                        return
                    dst = og[a[0]][:, a[1], :]
                else:
                    dst = {"dn_U": d_U, "dn_X": X, "dn_u": u_, "dn_w": wT, "dn_o": o_sb}[k][:, t, :]
                act.copy(dst, src).then_inc(bank_free[b], 1)

            def pv(step, layer):
                if step[1] != "m" and step[2] == step[3]:
                    b = 4
                    act.wait_ge(*full(("pv", step[1], step[2], 0), layer))
                    act.copy(og[step[1]][:, step[2], :], ps[b][:, :]).then_inc(bank_free[b], 1)

            def soft(step, layer):
                _, a, t = step
                n = 0 if a == "m" else 1 + a
                act.wait_ge(*after("vector", step, layer))
                for h in range(H):
                    s = Sc[t][:, h, :]
                    last = av(s, s, ACT.Exp, bias=nmx[:, n, t, h:h + 1], scale=scale_of(a), accum_out=den[:, n, t, h:h + 1])
                last.then_inc(part("scalar", step), 1)

            def d_c0(step, layer):
                act.wait_ge(*after("vector", step, layer))
                av(cexp, cexp, ACT.Exp).then_inc(part("scalar", step), 1)

            parts = {"prep": prep, "evict": evict, "evict_z": evict, "norm": norm, "xT": xT, "mT": mT, "latT": latT, "yT": yT_step, "lat_norm": lat_norm,
                     "dn_g0": dn_g0, "dn_gc": dn_gc, "dn_row": dn_row, "dn_fT": dn_fT, "pv": pv, "soft": soft, "d_c0": d_c0,
                     **dict.fromkeys(("tr", "pT", "dn_U", "dn_X", "dn_u", "dn_w", "dn_o"), copies)}
            act.dma_start(tab[:, P:TAB_COLS], tables[:, P:TAB_COLS]).then_inc(start["tab_loaded"], 16)
            act.dma_start(pos_i[:, :], positions.rearrange("b (t p) -> (b p) t", p=P), allow_slow_non_contiguous=True).then_inc(start["pos_loaded"], 16)
            act.wait_ge(start["angles"], 1)
            av(mixed[:, 0, 0:384], mixed[:, 0, 0:384], ACT.Sin).then_inc(start["sines"], 1)
            with act.Fori(0, DEPTH) as layer:
                for step in ORDER:
                    if step[0] in parts:
                        parts[step[0]](step, layer)

        @block.vector
        def _(dve):
            tt, ts, stt = nc.vector.tensor_tensor, nc.vector.tensor_scalar, nc.vector.scalar_tensor_tensor

            def own_next(ins, layer):
                seen["vector"] += 1
                ins.then_inc(own["vector"], 1)
                dve.wait_ge(own["vector"], layer * OWN["vector"] + seen["vector"])

            def prep(step, layer):
                u = step[1]
                what, i, hf, nk, n = UNITS[u]
                for p in range(PIECES):
                    a, b = piece(nk, p)
                    dve.wait_ge(hi_done, layer * (PIECES * NU) + PIECES * u + p + 1)
                    tt(view(w_lo, u % SPLIT, nk, n)[:, a:b, :], view(raw, u % RAW, nk, n)[:, a:b, :],
                       view(w_hi, u % SPLIT, nk, n)[:, a:b, :].bitcast(F32), ALU.subtract).then_inc(lo_done, 1)

            def evict(step, layer):
                u = step[1]
                what, i, hf, nk, n = UNITS[u]
                key = bank_unit(u)
                if what == "z":
                    dve.wait_ge(*after("scalar", step, layer))
                    for t in range(NT):
                        stt(z[:, t, :], z[:, t, :], 1.0, ps[t][:, 0:n], ALU.add, ALU.mult).then_inc(bank_free[t], 1)
                elif what == "branch":
                    dve.wait_ge(*block_taken(unit_of("gate", i), layer))
                    if i // 2 == A and i % 2 == 0:
                        dve.wait_ge(*after("scalar", ("norm",), layer))
                    for t in range(NT):
                        dve.wait_ge(*full(key, layer, t))
                        dst = mixed[:, t, (i % 2) * n:(i % 2 + 1) * n] if i // 2 == A else gate[:, t, :]
                        stt(dst, gate[:, t, :], 1.0, ps[t][:, 0:n], ALU.add, ALU.mult).then_inc(bank_free[t], 1)
                elif what == "out":
                    for t in range(NT):
                        dve.wait_ge(*full(key, layer, t))
                        c = slice(i * n, (i + 1) * n)
                        tt(xs[:, t, c], xs[:, t, c], ps[t][:, 0:n], ALU.add).then_inc(bank_free[t], 1)

            def load(step, layer):
                if DEPTH > 1:
                    dve.wait_ge(*layer_start(layer))
                ts(prm[:, 0:ROWS_CONV], prm_all[:, bass.ds(layer * PRM_ROWS, ROWS_CONV)], 0.5, None, ALU.mult)
                nc.vector.tensor_copy(prm[:, ROWS_CONV:], prm_all[:, bass.ds(layer * PRM_ROWS + ROWS_CONV, PRM_ROWS - ROWS_CONV)])\
                    .then_inc(part("vector", step), 1)

            def split_lo(step, layer, k0, dst, scale, n=2):
                b = banks(step)[0]
                dve.wait_ge(*after("scalar", step, layer))
                for j in range(n):
                    last = stt(dst[1][:, k0 + j, :], ps[b][:, j * S:(j + 1) * S], scale(k0 + j), dst[0][:, k0 + j, :].bitcast(F32),
                               ALU.mult, ALU.subtract)
                last.then_inc(bank_free[b], 1)

            def xT(step, layer):
                if step[1] == 0:
                    dve.wait_ge(*after("vector", ("load",), layer))
                split_lo(step, layer, 2 * step[1], hT, lambda c: prm[:, PRM_NORM + c:PRM_NORM + c + 1])

            def mT(step, layer):
                split_lo(step, layer, 2 * step[1], hT, lambda c: 0.5)

            def latT(step, layer):
                j = step[1]
                split_lo(step, layer, 2 * j, yT, lambda c: prm[:, PRM_LAT + c:PRM_LAT + c + 1], 2 if j < 2 else 1)

            def yT_step(step, layer):
                split_lo(step, layer, 2 * step[2], yT, lambda c: 1.0)

            def dn_g0(step, layer):
                dve.wait_ge(gains_loaded, layer * (7 * 16) + 7 * 16)
                dve.wait_ge(*block_taken(1, layer))
                own_next(tt(a1, ab[:, :, 0:H], gains("dt").unsqueeze(1).broadcast_to([P, NT, H]), ALU.add), layer)
                stt(na, a1, -1.0, a1, ALU.mult, ALU.min).then_inc(part("vector", step), 1)

            def dn_g1(step, layer):
                dve.wait_ge(*after("scalar", ("dn_g0",), layer))
                own_next(stt(rl, a1, 0.0, lnp, ALU.max, ALU.add), layer)
                ts(beta, bt, 0.5, 0.5, ALU.mult, ALU.add)
                stt(g_, rl, -1.0, ea.unsqueeze(1).broadcast_to([P, NT, H]), ALU.mult, ALU.mult).then_inc(part("vector", step), 1)

            def dn_gc(step, layer):
                dve.wait_ge(*full(step, layer))
                nc.vector.tensor_copy(gcs, ps[3][:, 0:NT * 16].rearrange("p (t n) -> p t n", t=NT)).then_inc(bank_free[3], 1)
                dve.wait_ge(*taken(step, layer))
                tt(gdiff, gcs[:, :, H:2 * H], gcs[:, :, 0:H], ALU.subtract).then_inc(part("vector", step), 1)

            def dn_row(step, layer):
                t = step[1]
                b = banks(step)[0]
                dve.wait_ge(*full(step, layer))
                tt(heads(d_D[:, t, :]), heads(ps[b][:, :]), per_head(gcs[:, t, 0:H]), ALU.subtract).then_inc(bank_free[b], 1)
                dve.wait_ge(*taken(step, layer))
                own_next(ts(d_Dt[:, t, :], d_D[:, t, :], 0.0, None, ALU.min), layer)
                ts(d_D[:, t, :], d_D[:, t, :], 0.0, None, ALU.max).then_inc(part("vector", step), 1)

            def dn_fT(step, layer):
                _, i, j = step
                b = banks(step)[0]
                dve.wait_ge(*full(step, layer))

                def tap(k, n):
                    c = (CONV - 1 - k) * (3 * H) + i * H + 2 * j + n
                    return prm[:, c:c + 1]

                for n in range(2):
                    ins = ts(feat[:, 2 * j + n, :], ps[b][:, n * S:(n + 1) * S], tap(0, n), None, ALU.mult)
                own_next(ins, layer)
                for k in range(1, CONV):
                    for n in range(2):
                        y = feat[:, 2 * j + n, k:S]
                        ins = stt(y, ps[b][:, n * S:(n + 1) * S - k], tap(k, n), y, ALU.mult, ALU.add)
                    if k < CONV - 1:
                        own_next(ins, layer)
                ins.then_inc(bank_free[b], 1)

            def dn_silu(step, layer):
                i = step[1]
                dve.wait_ge(*after("scalar", ("dn_fT", i, 1), layer))
                stt(conv, th, 1.0, conv, ALU.add, ALU.mult).then_inc(part("vector", step), 1)

            def dn_ss(step, layer):
                i = step[1]
                dve.wait_ge(*full(step, layer))
                ts(ssd[i], ps[3][:, 0:NT * H].rearrange("p (t n) -> p t n", t=NT), 1e-6, None, ALU.add).then_inc(bank_free[3], 1)

            def dn_bT(step, layer):
                _, i, t = step
                b = banks(step)[0]
                if i < 2 and t == 0:
                    dve.wait_ge(*after("gpsimd", ("dn_ss", i), layer))
                if i == 1 and t == 0:
                    dve.wait_ge(*full(("tr", "qg", 1), layer))
                dve.wait_ge(*full(step, layer))
                o = heads(ps[b][:, :])
                for dst, f in (((qn, rq), (qg, rqg)), ((kn, rk), (kbg, rkbg), (kdec, rkd)), ((vb, beta),))[i]:
                    last = tt(heads(dst[:, t, :]), o, per_head(f[:, t, :]), ALU.mult)
                last.then_inc(bank_free[b], 1)

            def dn_kk(step, layer):
                t = step[1]
                b = banks(step)[0]
                dve.wait_ge(*after("gpsimd", ("dn_row", t), layer))
                dve.wait_ge(*full(step, layer))
                tt(L[:, t, :], ps[b][:, :], d_D[:, t, :], ALU.mult).then_inc(bank_free[b], 1)

            def dn_qk(step, layer):
                t = step[1]
                b = banks(step)[0]
                dve.wait_ge(*full(step, layer))
                tt(Aqk[:, t, :], ps[b][:, :], d_Dt[:, t, :], ALU.mult).then_inc(bank_free[b], 1)

            def dn_TX(step, layer):
                _, s, t = step
                final = s == len(LEVELS) - 1
                for i, dst in enumerate((d_TT,) if final else (d_T, d_TT)):
                    b = banks(step)[i]
                    dve.wait_ge(*full(step, layer, i))
                    tt(dst[:, t, :], dst[:, t, :], ps[b][:, :], ALU.subtract).then_inc(bank_free[b], 1)

            def dn_v0(step, layer):
                dve.wait_ge(*taken(("dn_u", 0), layer))
                nc.vector.tensor_copy(vnew[0:CH, 0, :], u_[0:CH, 0, :]).then_inc(part("vector", step), 1)

            def dn_ws(step, layer):
                c = step[1]
                t, r = c // 2, slice(CH * (c % 2), CH * (c % 2) + CH)
                b = banks(step)[0]
                dve.wait_ge(*full(step, layer))
                tt(vnew[r, t, :], u_[r, t, :], ps[b][r, :], ALU.subtract).then_inc(bank_free[b], 1)

            def dn_ds(step, layer):
                c = step[1]
                b = banks(step)[0]
                dve.wait_ge(*full(step, layer))
                if c == 0:
                    nc.vector.tensor_copy(states[1], ps[b][:, :]).then_inc(bank_free[b], 1)
                else:
                    dve.wait_ge(*after("gpsimd", ("dn_dec", c), layer))
                    tt(states[c + 1], states[c + 1], ps[b][:, :], ALU.add).then_inc(bank_free[b], 1)

            def dn_o(step, layer):
                t = step[1]
                dve.wait_ge(*after("gpsimd", step, layer))
                nc.vector.tensor_reduce(oss[:, t, :], heads(o_sq[:, t, :]), AX.X, ALU.add).then_inc(part("vector", step), 1)

            def b_out(step, layer):
                dve.wait_ge(*after("gpsimd", ("dn_on",), layer))
                dve.wait_ge(*after("gpsimd", evict_step(unit_of("z", B)), layer))
                for t in range(NT):
                    last = tt(heads(o_sb[:, t, :]), heads(o_sb[:, t, :]), per_head(ors[:, t, :]), ALU.mult)
                own_next(last, layer)
                tt(z, z, o_sb, ALU.mult).then_inc(part("vector", step), 1)

            def q_norm(step, layer):
                dve.wait_ge(*after("gpsimd", step, layer))
                sq = at[:, 0:NT * H * QK].rearrange("p (t h d) -> p t h d", t=NT, h=H)
                nc.vector.tensor_reduce(hss[:, :, 0:H], sq[:, :, :, 0:HD], AX.X, ALU.add)
                nc.vector.tensor_reduce(hss[:, :, H:2 * H], sq[:, :, :, HD:QK], AX.X, ALU.add).then_inc(part("vector", step), 1)

            def q_rope(step, layer):
                t = step[1]
                dve.wait_ge(*after("gpsimd", ("q_rs",), layer))
                for h in range(H):
                    q = mq[:, t, h * QK:h * QK + HD]
                    last = stt(q, q, hrs[:, t, h:h + 1], gains("mq")[:, 0:HD], ALU.mult, ALU.mult)
                last.then_inc(part("vector", step), 1)

            def k_norm(step, layer):
                dve.wait_ge(*after("gpsimd", step, layer))
                sq = at[:, 0:NT * W].rearrange("p (t h d) -> p t h d", t=NT, h=H)
                nc.vector.tensor_reduce(hss[:, :, 2 * H:3 * H], sq, AX.X, ALU.add).then_inc(part("vector", step), 1)

            def k_rs(step, layer):
                dve.wait_ge(*after("gpsimd", step, layer))
                for t in range(NT):
                    for h in range(H):
                        k = kv[:, t, h * 2 * HD:h * 2 * HD + HD]
                        last = stt(k, k, hrs[:, t, 2 * H + h:2 * H + h + 1], gains("mk")[:, 0:HD], ALU.mult, ALU.mult)
                last.then_inc(part("vector", step), 1)

            def sc(step, layer):
                _, a, t, j = step
                b = banks(step)[0]
                nk = (t + 1) * P
                m = const(f"mask_{a}")[:, (1 - t) * P:2 * P]
                hs = slice(0, H) if t == 0 else slice(2 * j, 2 * j + 2)
                n = hs.stop - hs.start
                dve.wait_ge(*full(step, layer))
                tt(Sc[t][:, hs, :], ps[b][:, :].rearrange("p (h k) -> p h k", k=nk), m.unsqueeze(1).broadcast_to([P, n, nk]), ALU.add)\
                    .then_inc(bank_free[b], 1)

            def soft(step, layer):
                _, a, t = step
                n = 0 if a == "m" else 1 + a
                dve.wait_ge(*taken(("sc", a, t, t), layer))
                own_next(nc.vector.tensor_reduce(mx[:, n, t, :], Sc[t], AX.X, ALU.max), layer)
                ts(nmx[:, n, t, :], mx[:, n, t, :], -scale_of(a), None, ALU.mult).then_inc(part("vector", step), 1)

            def pv(step, layer):
                _, a, t, j = step
                if a != "m" or j != t:
                    return
                dve.wait_ge(*after("scalar", ("soft", a, t), layer))
                own_next(nc.vector.reciprocal(mr[:, t, :], den[:, 0, t, :]), layer)
                dve.wait_ge(*full(("pv", a, t, 0), layer))
                tt(heads(m_o[t]), heads(ps[4][:, :]), per_head(mr[:, t, :]), ALU.mult).then_inc(bank_free[4], 1)

            def m_out(step, layer):
                dve.wait_ge(*taken(("pv", "m", 1, 0), layer))
                dve.wait_ge(*after("gpsimd", evict_step(unit_of("z", A)), layer))
                for t in range(NT):
                    last = tt(z[:, t, :], z[:, t, :], m_o[t], ALU.mult)
                last.then_inc(part("vector", step), 1)

            def d_sq(step, layer):
                dve.wait_ge(*after("gpsimd", step, layer))
                nc.vector.tensor_reduce(dss, gate.rearrange("p t (h d) -> p t h d", h=H), AX.X, ALU.add).then_inc(part("vector", step), 1)

            def d_rope(step, layer):
                _, g, k = step
                name = "dq" if k == 0 else "dk"
                dve.wait_ge(*after("gpsimd", ("d_rs", g, k), layer))
                if g == 0 and k == 0:
                    dve.wait_ge(*after("gpsimd", ("d_tables",), layer))
                s4 = stg.rearrange("p t (h d) -> p t h d", h=H)
                g4 = gate.rearrange("p t (h d) -> p t h d", h=H)
                own_next(tt(g4, s4, rg[name][0].unsqueeze(2).broadcast_to([P, NT, H, HD]), ALU.mult), layer)
                tt(s4, s4, rg[name][1].unsqueeze(2).broadcast_to([P, NT, H, HD]), ALU.mult).then_inc(part("vector", step), 1)

            n3 = nmx.rearrange("p a t h -> p a (t h)")[:, 1:, :]
            d3 = den.rearrange("p a t h -> p a (t h)")[:, 1:, :]
            c3 = cexp.rearrange("p a t h -> p a (t h)")
            e3 = cden.rearrange("p a t h -> p a (t h)")

            def row(v):
                return v.rearrange("p t h -> p (t h)")

            def d_c0(step, layer):
                dve.wait_ge(*after("scalar", ("soft", 2, 1), layer))
                own_next(tt(row(cmax), n3[:, 0, :], n3[:, 1, :], ALU.min), layer)
                own_next(tt(row(cmax), row(cmax), n3[:, 2, :], ALU.min), layer)
                tt(c3, row(cmax).unsqueeze(1).broadcast_to([P, GROUPS, NT * H]), n3, ALU.subtract).then_inc(part("vector", step), 1)

            def d_c1(step, layer):
                dve.wait_ge(*after("scalar", ("d_c0",), layer))
                own_next(tt(e3, c3, d3, ALU.mult), layer)
                own_next(tt(row(csum), e3[:, 0, :], e3[:, 1, :], ALU.add), layer)
                own_next(tt(row(csum), row(csum), e3[:, 2, :], ALU.add), layer)
                own_next(nc.vector.reciprocal(row(csum), row(csum)), layer)
                tt(c3, c3, row(csum).unsqueeze(1).broadcast_to([P, GROUPS, NT * H]), ALU.mult).then_inc(part("vector", step), 1)

            def d_out(step, layer):
                dve.wait_ge(*after("vector", ("d_c1",), layer))
                dve.wait_ge(*taken(("pv", 2, 1, 0), layer))
                for a in range(2):
                    o = og[a].rearrange("p t (h d) -> p (t h) d", h=H)
                    last = tt(o, o, per_head(c3[:, a, :], h=NT * H), ALU.mult)
                own_next(last, layer)
                own_next(tt(og[0], og[0], og[1], ALU.add), layer)
                dve.wait_ge(*after("gpsimd", step, layer))
                own_next(tt(og[0], og[0], og[2], ALU.add), layer)
                dve.wait_ge(*after("gpsimd", evict_step(unit_of("z", C)), layer))
                tt(z, z, og[0], ALU.mult).then_inc(part("vector", step), 1)

            parts = {"prep": prep, **dict.fromkeys(("evict", "evict_z", "evict_first", "evict_branch"), evict), "load": load, "xT": xT, "mT": mT, "latT": latT, "yT": yT_step, "dn_g0": dn_g0,
                     "dn_g1": dn_g1, "dn_gc": dn_gc, "dn_row": dn_row, "dn_fT": dn_fT, "dn_silu": dn_silu, "dn_ss": dn_ss,
                     "dn_bT": dn_bT, "dn_kk": dn_kk, "dn_qk": dn_qk, "dn_TX": dn_TX, "dn_v0": dn_v0, "dn_ws": dn_ws, "dn_ds": dn_ds, "dn_o": dn_o,
                     "b_out": b_out, "q_norm": q_norm, "q_rope": q_rope, "k_norm": k_norm, "k_rs": k_rs, "sc": sc, "soft": soft,
                     "pv": pv, "m_out": m_out, "d_sq": d_sq, "d_rope": d_rope, "d_c0": d_c0, "d_c1": d_c1, "d_out": d_out}

            dve.wait_ge(start["pos_loaded"], 16)
            dve.wait_ge(start["tab_loaded"], 32)
            n_start = [0]

            def next_start(ins):
                n_start[0] += 1
                ins.then_inc(start["angle_step"], 1)
                dve.wait_ge(start["angle_step"], n_start[0])

            half = (ROPE + HD) // 2
            raw_angle = mixed[:, 1, 0:NT * half].rearrange("p (t n) -> p t n", t=NT)
            turns = mixed[:, 1, NT * half:2 * NT * half].rearrange("p (t n) -> p t n", t=NT)
            next_start(nc.vector.tensor_copy(pos_f, pos_i[:, :]))
            for t in range(NT):
                last = ts(raw_angle[:, t, :], const("inv"), pos_f[:, t:t + 1], None, ALU.mult)
            next_start(last)
            for i in range(2):
                r = mixed[:, 0, i * NT * half:(i + 1) * NT * half].rearrange("p (t n) -> p t n", t=NT)
                next_start(ts(turns, raw_angle, 1.0 / TWO_PI, 0.25 * i, ALU.mult, ALU.add))
                next_start(ts(turns, turns, ROUND, None, ALU.add))
                next_start(ts(turns, turns, ROUND, None, ALU.subtract))
                next_start(stt(r, turns, -TWO_PI_PARTS[0], raw_angle, ALU.mult, ALU.add))
                next_start(stt(r, turns, -TWO_PI_PARTS[1], r, ALU.mult, ALU.add))
                next_start(stt(r, turns, -TWO_PI_PARTS[2], r, ALU.mult, ALU.add))
                next_start(ts(r, r, 0.5 * np.pi * i, PI_BELOW, ALU.add, ALU.min))
                last = ts(r, r, -PI_BELOW, None, ALU.max)
                if i == 0:
                    next_start(last)
            last.then_inc(start["angles"], 1)
            dve.wait_ge(start["sines"], 1)
            first = {ROPE: 0, HD: ROPE // 2}
            for n in (ROPE, HD):
                for i, (o, f) in enumerate(((NT * half, 1.0), (0, 1.0))):
                    v = mixed[:, 0, o:o + NT * half].rearrange("p (t n) -> p t n", t=NT)[:, :, first[n]:first[n] + n // 2]
                    ts(rot[n][i][:, :, 0:n // 2], v, 1.0, None, ALU.mult)
                    last = ts(rot[n][i][:, :, n // 2:n], v, 1.0 if i == 0 else -1.0, None, ALU.mult)
            last.then_inc(start["rot_ready"], 1)
            dve.wait_ge(start["rows_T"], 1)
            nc.vector.tensor_copy(prm_all[:, :], ps[7][:, 0:DEPTH * PRM_ROWS]).then_inc(start["rows_copied"], 1)
            dve.wait_ge(start["rows_copied"], 1)
            with dve.Fori(0, DEPTH) as layer:
                for step in ORDER:
                    if step[0] in parts:
                        parts[step[0]](step, layer)

        @block.gpsimd
        def _(pool):
            tt = nc.gpsimd.tensor_tensor

            def tc(dst, src, name, op):
                c = const(name)
                for _ in range(len(src.shape) - 2):
                    c = c.unsqueeze(1)
                return tt(dst, src, c.broadcast_to(list(src.shape)), op)

            def own_next(ins, layer):
                seen["gpsimd"] += 1
                ins.then_inc(own["gpsimd"], 1)
                pool.wait_ge(own["gpsimd"], layer * OWN["gpsimd"] + seen["gpsimd"])

            def inverse_root(dst, src, scale, layer):
                own_next(tc(dst, src, scale, ALU.mult), layer)
                own_next(tc(dst, dst, "eps", ALU.add), layer)
                return tc(dst, dst, "power", ALU.pow)

            def evict(step, layer):
                u = step[1]
                what, i, hf, nk, n = UNITS[u]
                if what == "z":
                    pool.wait_ge(*block_taken(u, layer))
                    for t in range(NT):
                        last = tt(z[:, t, :], z[:, t, :], hrstd[:, t:t + 1].broadcast_to([P, W]), ALU.mult)
                    if i == B:
                        own_next(last, layer)
                        last = tt(z.rearrange("p t (h d) -> p (t h) d", h=H), z.rearrange("p t (h d) -> p (t h) d", h=H),
                                  gains("dn").unsqueeze(1).broadcast_to([P, NT * H, HD]), ALU.mult)
                    last.then_inc(part("gpsimd", step), 1)
                else:
                    pool.wait_ge(*block_taken(u, layer))
                    m = mixed[:, :, (i % 2) * n:(i % 2 + 1) * n]
                    tt(m, m, gate, ALU.add).then_inc(part("gpsimd", step), 1)

            def norm(step, layer):
                pool.wait_ge(*after("scalar", step, layer))
                own_next(inverse_root(rstd, ss_x, "inv_d", layer), layer)
                tc(hrstd, rstd, "half", ALU.mult).then_inc(part("gpsimd", step), 1)

            def tables_of(names, step, layer):
                for name in names:
                    n = ROPE if name[0] == "m" else HD
                    gn = gains(name)[:, -n:]
                    for i in range(2):
                        last = tt(rg[name][i], rot[n][i], gn.unsqueeze(1).broadcast_to([P, NT, n]), ALU.mult)
                last.then_inc(part("gpsimd", step), 1)

            def m_tables(step, layer):
                pool.wait_ge(gains_loaded, layer * (7 * 16) + 7 * 16)
                pool.wait_ge(start["rot_ready"], 1)
                tables_of(("mq", "mk"), step, layer)

            def d_tables(step, layer):
                pool.wait_ge(*after("vector", ("m_out",), layer))
                pool.wait_ge(*full(("pv", "m", 1, 0), layer))
                tables_of(("dq", "dk"), step, layer)

            def lat_norm(step, layer):
                pool.wait_ge(*after("scalar", step, layer))
                own_next(tt(lrs, lss, const("inv_n").unsqueeze(1).broadcast_to([P, NT, 3]), ALU.mult), layer)
                own_next(tc(lrs, lrs, "eps", ALU.add), layer)
                tc(lrs, lrs, "power", ALU.pow).then_inc(part("gpsimd", step), 1)

            def rotate(v, name, h, scale, t, layer):
                x, y = (gate[:, t, i * H * ROPE:(i * H + h) * ROPE].rearrange("p (h d) -> p h d", h=h) for i in range(2))
                c, s = (rg[name][i][:, t, :].unsqueeze(1).broadcast_to([P, h, ROPE]) for i in range(2))
                own_next(tt(v, v, scale, ALU.mult), layer)
                tt(x, v, c, ALU.mult)
                own_next(tt(y, v, s, ALU.mult), layer)
                n = ROPE // 2
                tt(v[:, :, 0:n], x[:, :, 0:n], y[:, :, n:ROPE], ALU.add)
                return tt(v[:, :, n:ROPE], x[:, :, n:ROPE], y[:, :, 0:n], ALU.add)

            def kpe(step, layer):
                pool.wait_ge(*after("gpsimd", ("lat_norm",), layer))
                pool.wait_ge(*layer_start(layer))
                for t in range(NT):
                    v = lat[:, t, Q_RANK + KV_RANK:].unsqueeze(1)
                    last = rotate(v, "mk", 1, per_head(lrs[:, t, 2:3], ROPE, 1), t, layer)
                last.then_inc(part("gpsimd", step), 1)

            def q_norm(step, layer):
                pool.wait_ge(*block_taken(unit_of("qb", 1), layer))
                pool.wait_ge(*after("scalar", ("lat_norm",), layer))
                m = mq.rearrange("p t n -> p (t n)")
                tt(at[:, 0:NT * H * QK], m, m, ALU.mult).then_inc(part("gpsimd", step), 1)

            def q_rs(step, layer):
                pool.wait_ge(*after("vector", ("q_norm",), layer))
                inverse_root(hrs[:, :, 0:H], hss[:, :, 0:H], "inv_hd", layer)
                inverse_root(hrs[:, :, H:2 * H], hss[:, :, H:2 * H], "inv_rope", layer).then_inc(part("gpsimd", step), 1)

            def q_rope(step, layer):
                t = step[1]
                pool.wait_ge(*after("gpsimd", ("q_rs",), layer))
                pool.wait_ge(*after("gpsimd", ("kpe",), layer))
                v = mq[:, t, :].rearrange("p (h d) -> p h d", h=H)[:, :, HD:QK]
                rotate(v, "mq", H, per_head(hrs[:, t, H:2 * H], ROPE), t, layer).then_inc(part("gpsimd", step), 1)

            def k_norm(step, layer):
                pool.wait_ge(*block_taken(unit_of("kvb", 1), layer))
                pool.wait_ge(*after("vector", ("q_norm",), layer))
                k = kv.rearrange("p t (h d) -> p t h d", h=H)[:, :, :, 0:HD]
                sq = at[:, 0:NT * W].rearrange("p (t h d) -> p t h d", t=NT, h=H)
                for t in range(NT):
                    last = tt(sq[:, t], k[:, t], k[:, t], ALU.mult)
                last.then_inc(part("gpsimd", step), 1)

            def k_rs(step, layer):
                pool.wait_ge(*after("vector", ("k_norm",), layer))
                inverse_root(hrs[:, :, 2 * H:3 * H], hss[:, :, 2 * H:3 * H], "inv_hd", layer).then_inc(part("gpsimd", step), 1)

            def dn_gc(step, layer):
                pool.wait_ge(*after("scalar", step, layer))
                tt(begc, beta, egc, ALU.mult).then_inc(part("gpsimd", step), 1)

            def dn_row(step, layer):
                t = step[1]
                pool.wait_ge(*after("scalar", step, layer))
                own_next(tt(heads(d_D[:, t, :]), heads(d_D[:, t, :]), over_heads(const("strict")), ALU.mult), layer)
                tt(heads(d_Dt[:, t, :]), heads(d_Dt[:, t, :]), over_heads(const("tri")), ALU.mult)
                tt(heads(d_D[:, t, :]), heads(d_D[:, t, :]), per_head(beta[:, t, :]), ALU.mult).then_inc(part("gpsimd", step), 1)

            def dn_sq(step, layer):
                pool.wait_ge(*after("vector", ("dn_silu", step[1]), layer))
                tt(th, conv, conv, ALU.mult).then_inc(part("gpsimd", step), 1)

            def dn_ss(step, layer):
                i = step[1]
                pool.wait_ge(*taken(step, layer))
                r = (rq, rk)[i]
                own_next(tc(r, ssd[i], "power", ALU.pow), layer)
                if i == 0:
                    own_next(tc(rq, rq, "q_scale", ALU.mult), layer)
                    pool.wait_ge(*after("scalar", ("dn_gc",), layer))
                    last = tt(rqg, rq, egc, ALU.mult)
                else:
                    tt(rkbg, rk, begc, ALU.mult)
                    last = tt(rkd, rk, edec, ALU.mult)
                last.then_inc(part("gpsimd", step), 1)

            def dn_U(step, layer):
                t = step[1]
                pool.wait_ge(*taken(step, layer))
                own_next(tt(heads(d_T[:, t, :]), heads(L[:, t, :]), over_heads(const("level")), ALU.mult), layer)
                own_next(tt(heads(d_TT[:, t, :]), heads(d_U[:, t, :]), over_heads(const("levelT1")), ALU.mult), layer)
                tt(heads(d_T[:, t, :]), over_heads(ident), heads(d_T[:, t, :]), ALU.subtract)
                tt(heads(d_TT[:, t, :]), over_heads(ident), heads(d_TT[:, t, :]), ALU.subtract).then_inc(part("gpsimd", step), 1)

            def dn_M(step, layer):
                _, s, t = step
                pool.wait_ge(*(taken(("dn_U", t), layer) if s == 1 else full(("dn_X", s - 1, t), layer)))
                tt(heads(d_Us[:, t, :]), heads(d_U[:, t, :]), over_heads(const(f"levelT{LEVELS[s]}")), ALU.mult)\
                    .then_inc(part("gpsimd", step), 1)

            def dn_dec(step, layer):
                c = step[1]
                pool.wait_ge(*taken(("dn_ds", c - 1), layer))
                e = eS[:, c // 2, (c % 2) * H:(c % 2 + 1) * H]
                tt(heads(states[c + 1]), heads(states[c]), per_head(e), ALU.mult).then_inc(part("gpsimd", step), 1)

            def dn_o(step, layer):
                t = step[1]
                pool.wait_ge(*taken(step, layer))
                tt(o_sq[:, t, :], o_sb[:, t, :], o_sb[:, t, :], ALU.mult).then_inc(part("gpsimd", step), 1)

            def dn_on(step, layer):
                pool.wait_ge(*after("vector", ("dn_o", 1), layer))
                inverse_root(ors, oss, "inv_hd", layer)\
                    .then_inc(part("gpsimd", step), 1)

            def d_sq(step, layer):
                _, g, k = step
                i = 3 * g + k
                pool.wait_ge(*block_taken(unit_of("dil", i), layer))
                if i > 0:
                    pool.wait_ge(*full(("tr", "dq", 2 * g + 1) if k else ("tr", "dk", 2 * g - 1), layer))
                tt(gate, stg, stg, ALU.mult).then_inc(part("gpsimd", step), 1)

            def d_rs(step, layer):
                _, g, k = step
                pool.wait_ge(*after("vector", ("d_sq", g, k), layer))
                own_next(inverse_root(drs, dss, "inv_hd", layer), layer)
                s = stg.rearrange("p t (h d) -> p (t h) d", h=H)
                tt(s, s, per_head(drs.rearrange("p t h -> p (t h)"), h=NT * H), ALU.mult).then_inc(part("gpsimd", step), 1)

            def d_rope(step, layer):
                pool.wait_ge(*after("vector", step, layer))
                n = HD // 2
                x = gate.rearrange("p t (h d) -> p (t h) d", h=H)
                v = stg.rearrange("p t (h d) -> p (t h) d", h=H)
                tt(x[:, :, 0:n], x[:, :, 0:n], v[:, :, n:HD], ALU.add)
                tt(x[:, :, n:HD], x[:, :, n:HD], v[:, :, 0:n], ALU.add).then_inc(part("gpsimd", step), 1)

            def d_out(step, layer):
                pool.wait_ge(*after("vector", ("d_c1",), layer))
                pool.wait_ge(*taken(("pv", 2, 1, 0), layer))
                o = og[2].rearrange("p t (h d) -> p (t h) d", h=H)
                tt(o, o, per_head(cexp[:, 2].rearrange("p t h -> p (t h)"), h=NT * H), ALU.mult).then_inc(part("gpsimd", step), 1)

            parts = {"evict_z": evict, "evict_branch": evict, "norm": norm, "m_tables": m_tables, "d_tables": d_tables, "lat_norm": lat_norm, "kpe": kpe,
                     "q_norm": q_norm, "q_rs": q_rs, "q_rope": q_rope, "k_norm": k_norm, "k_rs": k_rs, "dn_gc": dn_gc,
                     "dn_row": dn_row, "dn_sq": dn_sq, "dn_ss": dn_ss, "dn_U": dn_U, "dn_M": dn_M,
                     "dn_dec": dn_dec, "dn_o": dn_o, "dn_on": dn_on, "d_sq": d_sq, "d_rs": d_rs, "d_rope": d_rope, "d_out": d_out}
            pool.wait_ge(start["tab_loaded"], 32)
            with pool.Fori(0, DEPTH) as layer:
                for step in ORDER:
                    if step[0] in parts:
                        parts[step[0]](step, layer)

        assert seen == OWN, f"OWN = {seen}"


def kernel(**inputs):
    import concourse.bacc as bacc
    from concourse.bass_utils import run_bass_kernel_spmd

    names = ["x", "positions", "norm_g", "w_in", "mla_q_a_norm_g", "mla_w_q_b", "mla_kv_a_norm_g", "mla_w_kv_b",
             "mla_q_norm_g", "mla_k_norm_g", "dn_conv_w", "dn_a_log", "dn_dt_bias", "dn_out_norm_g",
             "dil_q_norm_g", "dil_k_norm_g", "w_branch", "w_out"]
    nc = bacc.Bacc("TRN2", target_bir_lowering=False, num_devices=1)
    arrays = {name: np.ascontiguousarray(inputs[name]) for name in names}
    arrays["tables"] = shape_tables()
    args = [nc.dram_tensor(f"in_{name}", a.shape, mybir.dt.from_np(a.dtype), kind="ExternalInput").ap() for name, a in arrays.items()]
    args.append(nc.dram_tensor("out", arrays["x"].shape, F32, kind="ExternalOutput").ap())
    hybrid_trunk(nc, *args)
    r = run_bass_kernel_spmd(nc, [{f"in_{name}": a for name, a in arrays.items()}], core_ids=[0])
    return r.results[0]["out"]
```

```python
from contextlib import ExitStack

import numpy as np

import concourse.bass as bass
from concourse import mybir

ALU = mybir.AluOpType
ACT = mybir.ActivationFunctionType
AX = mybir.AxisListType
F32 = mybir.dt.float32
F32R = mybir.dt.float32r
I32 = mybir.dt.int32

P = 128
NT = 2
S = NT * P
D = 1024
KC = D // P
H = 4
HD = 128
W = H * HD
CH = 64
DEPTH = 2
EPS = 1e-6
NEG = -1e30
Q_RANK, KV_RANK, ROPE = 384, 256, 64
QK = HD + ROPE
CONV = 4
GROUPS = 3
DILATIONS = (1, 4, 16)
BRANCHES = 3
LEVELS = (1, 2, 4, 8, 16, 32)
PIECES = 2

COL, _at = {}, 0
for _name, _n in (("q_lat", Q_RANK), ("kv_lat", KV_RANK + ROPE), ("z0", W), ("dn", 3 * W), ("ab", 2 * H),
                  ("z1", W), ("dil", 3 * GROUPS * W), ("z2", W), ("gate", BRANCHES * D)):
    COL[_name] = _at
    _at += _n
IN_WIDTH = _at
A, B, C = 0, 1, 2
TWO_PI = 2.0 * np.pi
TWO_PI_PARTS = [6.28125]
TWO_PI_PARTS.append(float((np.float32(TWO_PI - 6.28125).view(np.uint32) & np.uint32(0xFFFFE000)).view(np.float32)))
TWO_PI_PARTS.append(float(np.float32(TWO_PI - sum(TWO_PI_PARTS))))
PI_BELOW = float(np.nextafter(np.float32(np.pi), np.float32(0)))
ROUND = 1.5 * 2.0 ** 23


def unit_list():
    def halves(what, i, n):
        return [(what, i, hf, KC // 2, n) for hf in range(2)]

    def merged(n, c):
        return (halves("z", n, W) if c == 0 else []) + halves("gate", 2 * n + c, 512) + [("branch", 2 * n + c, 0, W // P, 512)]

    us = halves("latq", 0, Q_RANK + 2 * H) + halves("latkv", 0, KV_RANK + ROPE) + halves("dn", 0, W)
    us += [("qb", j, 0, Q_RANK // P, 2 * QK) for j in range(2)] + halves("dn", 1, W)
    us += [("kvb", j, 0, KV_RANK // P, 4 * HD) for j in range(2)] + halves("dn", 2, W)
    dil = [halves("dil", i, W) for i in range(3 * GROUPS)]
    us += merged(A, 0)[:2] + dil[0] + merged(A, 0)[2:]
    for d in dil[1:]:
        us += d
    us += merged(A, 1)
    for n in (C, B):
        us += merged(n, 0) + merged(n, 1)
    return us + halves("out", 0, 512) + halves("out", 1, 512)


UNITS = unit_list()
NU = len(UNITS)
RAW, SPLIT = 3, 2
assert NU % RAW == 0 and NU % SPLIT == 0


def step_table():
    st = {u: [] for u in range(-1, NU)}

    def put(u, *steps):
        st[u] += steps

    put(-1, ("load",), *[("xT", k) for k in range(4)], ("norm",), ("m_tables",))
    put(1, ("dn_g0",), ("dn_g1",))
    put(2, ("dn_gc",))
    put(3, ("lat_norm",))
    put(4, ("latT", 0), ("latT", 1), ("latT", 2))
    put(5, ("kpe",), ("dn_fT", 0, 0))
    put(6, ("dn_fT", 0, 1))
    put(7, ("q_rs",), ("dn_th", 0), ("dn_silu", 0))
    put(8, ("q_rope", 0), ("q_rope", 1), ("dn_sq", 0))
    put(9, ("tr", "mqn", 0), ("tr", "mqn", 1), ("dn_ss", 0))
    put(10, ("tr", "mqp", 0), ("tr", "mqp", 1), ("dn_bT", 0, 0), ("dn_bT", 0, 1))
    put(11, ("dn_fT", 1, 0), ("k_rs",), ("tr", "mkp", 0))
    put(12, ("tr", "mkn", 0), ("tr", "mkn", 1), ("dn_fT", 1, 1))
    put(13, *scores("m", 0), ("tr", "q", 0), ("tr", "q", 1), ("dn_th", 1), ("dn_silu", 1))
    put(14, ("dn_sq", 1), *scores("m", 1), ("tr", "qg", 0), ("tr", "qg", 1), ("pT", "m", 0, 0))
    put(15, ("pv", "m", 0, 0), ("pT", "m", 1, 0), ("dn_ss", 1))
    put(16, ("pv", "m", 1, 0), ("pT", "m", 1, 1), ("dn_bT", 1, 0), ("dn_bT", 1, 1))
    put(17, ("pv", "m", 1, 1), ("m_out",), ("d_tables",), ("dn_fT", 2, 0), ("tr", "k", 1))
    put(18, ("yT", A, 0), ("yT", A, 1), ("dn_fT", 2, 1), ("tr", "k", 0))
    put(19, ("dn_th", 2), ("dn_silu", 2), ("dn_row", 0))
    put(20, ("dn_decay", 0), ("dn_row", 1))
    put(21, ("dn_decay", 1), ("dn_kk", 0), ("dn_bT", 2, 0), ("dn_bT", 2, 1))
    put(22, ("dn_kk", 1), ("dn_qk", 0), ("dn_qk", 1))
    put(23, ("dn_U", 0), ("dn_M", 1, 0), ("dn_U", 1), ("dn_M", 1, 1))
    for s in range(1, len(LEVELS)):
        u = 21 + 3 * s + (s == 1)
        put(u, ("dn_X", s, 0), ("dn_X", s, 1))
        put(u + 1, ("dn_TX", s, 0))
        if s < len(LEVELS) - 1:
            put(u + 1, ("dn_M", s + 1, 0), ("dn_M", s + 1, 1))
        put(u + (2 if 1 < s < len(LEVELS) - 1 else 1), ("dn_TX", s, 1))
    put(38, ("dn_u", 0), ("dn_u", 1), ("dn_v0",))
    put(39, ("dn_w", 0), ("dn_w", 1))
    put(40, ("dn_ds", 0))
    put(41, ("dn_ws", 1), ("dn_dec", 1))
    put(42, ("dn_ds", 1))
    put(43, ("dn_ws", 2), ("dn_dec", 2))
    put(44, ("dn_ds", 2))
    put(45, ("dn_ws", 3))
    put(46, ("dn_o", 0), ("dn_o", 1), ("dn_on",))
    for g in range(GROUPS):
        b = 20 + 6 * g
        put(b, ("d_rs", g, 0), ("d_rope", g, 0))
        put(b + 2, ("tr", "dq", 2 * g), ("tr", "dq", 2 * g + 1), ("d_rs", g, 1), ("d_rope", g, 1))
        put(b + 4, ("tr", "dk", 2 * g), ("tr", "dk", 2 * g + 1))
        put(b + 5, *scores(g, 0))
        put(b + 6, *scores(g, 1))
        put(b + 6, ("pT", g, 0, 0))
        put(b + 7, ("pv", g, 0, 0), ("pT", g, 1, 0))
        put(b + 8, ("pv", g, 1, 0), ("pT", g, 1, 1))
        put(b + 9, ("pv", g, 1, 1))
    put(39, ("d_c0",), ("d_c1",))
    put(40, ("d_sum",))
    put(41, ("d_out",))
    put(42, ("yT", C, 0), ("yT", C, 1))
    put(49, ("b_out",))
    put(50, ("yT", B, 0), ("yT", B, 1))
    put(54, ("mT", 0), ("mT", 1))
    put(56, ("mT", 2), ("mT", 3))
    return st


def scores(a, t):
    return [("sc", a, t, j) for j in range(t + 1)] + [("soft", a, t)]


def whole(u):
    return UNITS[u][0] in ("qb", "kvb", "branch")


def evict_step(u):
    what, i = UNITS[u][:2]
    return ({"z": "evict_z", "branch": "evict_branch" if i // 2 != A else "evict_first"}.get(what, "evict"), u)


STEPS = step_table()
ORDER = [("prep", 0), *STEPS[-1]]
for _u in range(NU):
    ORDER.append(("unit", _u))
    if _u + 1 < NU:
        ORDER.append(("prep", _u + 1))
    if whole(_u) or UNITS[_u][2] == 1:
        ORDER.append(evict_step(_u))
    ORDER += STEPS[_u]


def banks(step):
    k, *a = step
    if k == "unit":
        what, _, hf, _, _ = UNITS[a[0]]
        return [0, 1] if hf == 0 else []
    if k in ("xT", "mT"):
        return [4 + a[0]]
    if k == "latT":
        return [5 + a[0]]
    if k == "yT":
        return [4 + a[1] * 3]
    if k == "tr":
        return [{"q": 2, "qg": 2, "k": 2, "mqn": 5, "mqp": 5, "mkn": 5, "mkp": 7, "dq": 5, "dk": 5}[a[0]] + a[1] % 2]
    if k == "sc":
        return [5 + (a[2] if a[1] else 0)]
    if k == "pT":
        return [7]
    if k == "pv":
        return [4] if a[2] == 0 else []
    if k in ("dn_fT", "dn_bT"):
        return [2 + a[1]]
    if k in ("dn_gc", "dn_ss"):
        return [3]
    if k in ("dn_row", "dn_kk", "dn_qk", "dn_U", "dn_u", "dn_w", "dn_o"):
        return [2 + a[0]]
    if k == "dn_X":
        return [2 + a[1]]
    if k == "dn_TX":
        return [2, 3] if a[0] < len(LEVELS) - 1 else [2 + a[1]]
    if k == "dn_ws":
        return [2]
    if k == "dn_ds":
        return [3]
    return []


TURN, TURNS = {}, [0] * 8
for _s in ORDER:
    for _b in banks(_s):
        TURN[(_s, _b)] = TURNS[_b]
        TURNS[_b] += 1

RAW_AT, RAW_TOTAL = [], [0] * RAW
for _u in range(NU):
    RAW_TOTAL[_u % RAW] += 2 if UNITS[_u][0] == "latq" else 1
    RAW_AT.append(RAW_TOTAL[_u % RAW])

COUNT, PLACE = {}, {}
for _s in ORDER:
    PLACE[_s] = COUNT.get(_s[0], 0)
    COUNT[_s[0]] = PLACE[_s] + 1
HALVES = sum(UNITS[_u][2] == 0 and not whole(_u) for _u in range(NU))
GATES = [u[1] for u in UNITS if u[0] == "gate" and u[2] == 0]
OWN = {"vector": 46, "scalar": 21, "gpsimd": 41}

TAB, _at = {}, 0
for _name, _n in (("ident", P), ("inv", ROPE // 2 + HD // 2),
                  ("inv_n", GROUPS), ("inv_d", 1), ("inv_hd", 1), ("inv_rope", 1), ("eps", 1), ("eps_hd", 1), ("half", 1), ("q_scale", 1),
                  ("power", 1), ("chunk", 2), ("one", 1), ("tri", P), ("same", P), ("strict", P), ("level", P),
                  *[(f"levelT{s}", P) for s in LEVELS], *[(f"mask_{a}", 2 * P) for a in ("m", 0, 1, 2)]):
    TAB[_name] = (_at, _n)
    _at += _n
TAB_COLS = _at
TAB_FIRST = TAB["tri"][0]
GAIN, _at = {}, 0
for _name, _n in (("mq", QK), ("mk", QK), ("dq", HD), ("dk", HD), ("dn", HD), ("a_log", H), ("dt", H)):
    GAIN[_name] = (_at, _n)
    _at += _n
GAIN_COLS = _at
ROWS_CONV, ROWS_NORM = CONV * 3 * H, KC
PRM_NORM, PRM_LAT = ROWS_CONV, ROWS_CONV + ROWS_NORM
PRM_ROWS = PRM_LAT + Q_RANK // P + KV_RANK // P


def shape_tables():
    i, j = np.arange(P)[:, None], np.arange(P)[None, :]
    same = i // CH == j // CH
    t = np.zeros((P, TAB_COLS), np.float32)

    def put(name, v):
        a, n = TAB[name]
        t[:, a:a + n] = v

    put("ident", i == j)
    put("tri", same & (i <= j))
    put("same", same)
    put("strict", same & (j < i))

    def level(s, r, c):
        return (r // (2 * s) == c // (2 * s)) & (r // s % 2 == 1) & (c // s % 2 == 0)

    put("level", level(1, i, j))
    for s in LEVELS:
        put(f"levelT{s}", level(s, j, i))
    for a, dil, prev in (("m", 1, i == i), (0, DILATIONS[0], j >= i), (1, DILATIONS[1], i == i), (2, DILATIONS[2], i == i)):
        ok = np.concatenate([prev & ((P + i - j) % dil == 0), (j <= i) & ((i - j) % dil == 0)], axis=1)
        put(f"mask_{a}", np.where(ok, 0.0, NEG))
    put("chunk", np.arange(P)[:, None] // CH == np.arange(2)[None, :])
    put("one", 1.0)
    theta = np.float32(10000.0)
    put("inv", np.concatenate([np.float32(1.0) / theta ** (np.arange(0, n, 2, dtype=np.float32) / np.float32(n)) for n in (ROPE, HD)])[None])
    put("inv_n", np.array([1.0 / Q_RANK, 1.0 / KV_RANK, 1.0 / ROPE], np.float32)[None])
    for name, v in (("inv_d", 1.0 / D), ("inv_hd", 1.0 / HD), ("inv_rope", 1.0 / ROPE), ("eps", EPS), ("eps_hd", EPS * HD), ("half", 0.5),
                    ("q_scale", HD ** -0.5), ("power", -0.5)):
        put(name, v)
    return t


def hybrid_trunk(nc, x, positions, norm_g, w_in, mla_q_a_norm_g, mla_w_q_b, mla_kv_a_norm_g, mla_w_kv_b,
                 mla_q_norm_g, mla_k_norm_g, dn_conv_w, dn_a_log, dn_dt_bias, dn_out_norm_g,
                 dil_q_norm_g, dil_k_norm_g, w_branch, w_out, tables, out):
    with ExitStack() as ctx:
        def sb(name, cols, dt=F32, rows=P):
            return ctx.enter_context(nc.sbuf_tensor(name, [rows, cols], dt))

        def sem(name):
            return ctx.enter_context(nc.semaphore(name))

        def v3(ap, a):
            return ap.rearrange("p (a b) -> p a b", a=a)

        tab = sb("tab", TAB_COLS)
        xs = v3(sb("xs", NT * D)[:, :], NT)
        gain = sb("gain", GAIN_COLS)
        prm_all = sb("prm_all", DEPTH * PRM_ROWS)
        prm = sb("prm", PRM_ROWS)
        rot = {n: [v3(sb(f"rot{n}{i}", NT * n)[:, :], NT) for i in range(2)] for n in (ROPE, HD)}
        raw = sb("raw", RAW * 2048)
        w_hi, w_lo = sb("w_hi", SPLIT * 2048, F32R), sb("w_lo", SPLIT * 2048, F32R)
        hT = [v3(sb(f"hT{i}", KC * S, F32R)[:, :], KC) for i in range(2)]
        yT = [v3(sb(f"yT{i}", 5 * S, F32R)[:, :], 5) for i in range(2)]
        gate = v3(sb("gate", NT * 512)[:, :], NT)
        mixed = v3(sb("mixed", NT * D)[:, :], NT)
        z = v3(sb("z", NT * W)[:, :], NT)
        dn = sb("dn", 10 * NT * W)
        at = sb("at", 10880)
        prm_rows = at[0:PRM_ROWS, 0:DEPTH * P]
        sm = sb("sm", 640)

        def dnbuf(i):
            return v3(dn[:, i * NT * W:(i + 1) * NT * W], NT)

        def heads(ap):
            return ap.rearrange("p (h d) -> p h d", h=H)

        mix = d_D = dnbuf(0)
        conv = d_U = dnbuf(1)
        th = d_Dt = dnbuf(2)
        d_T = dnbuf(3)
        kn = dnbuf(3)
        qT = d_TT = dnbuf(4)
        kT = d_Us = dnbuf(5)
        qgT = dnbuf(6)
        qg = kbg = dnbuf(7)
        qn = kdec = dnbuf(8)
        vb = dnbuf(9)
        L, Aqk, X = d_D, d_Dt, d_D
        u_, wT, vnew = d_T, d_U, X
        states = [None] + [dn[:, (4 + i // 2) * NT * W + (i % 2) * W:(4 + i // 2) * NT * W + (i % 2 + 1) * W] for i in range(3)]
        o_sb = kbg
        o_sq = vb
        feat = conv.rearrange("p t n -> p (t n)").rearrange("p (f s) -> p f s", f=H)
        th_f = th.rearrange("p t n -> p (t n)").rearrange("p (f s) -> p f s", f=H)

        off = [0]

        def atb(cols, back=None):
            a = off[0] if back is None else back
            off[0] = a + cols
            return at[:, a:a + cols]

        Sc = [v3(atb((t + 1) * H * P), H) for t in range(NT)]
        PT = v3(atb(1024), 2)
        base = off[0]
        lat = v3(atb(NT * (Q_RANK + KV_RANK + ROPE)), NT)
        mq = v3(atb(NT * H * QK), NT)
        kv = v3(atb(NT * H * 2 * HD), NT)
        mqnT, mqpT, mknT = (v3(atb(1024), H) for _ in range(3))
        mkpT = atb(S)
        assert off[0] <= 10880, off
        off[0] = base
        stg = v3(atb(1024), NT)
        dqT, dkT = (v3(atb(1024), H) for _ in range(2))
        dv = v3(atb(1024), NT)
        rg = {k: [v3(atb(NT * HD), NT) for _ in range(2)] for k in ("dq", "dk")}
        og = [v3(atb(1024), NT) for _ in range(GROUPS)]
        assert off[0] <= 10880, off
        spare = mixed[:, 1, D - 4 * NT * ROPE:]
        rg.update({k: [v3(spare[:, (2 * n + i) * NT * ROPE:(2 * n + i + 1) * NT * ROPE], NT) for i in range(2)]
                   for n, k in enumerate(("mq", "mk"))})

        m_o = [mq.rearrange("p t n -> p (t n)")[:, t * W:(t + 1) * W] for t in range(NT)]

        so = [0]

        def small(n):
            so[0] += n
            assert so[0] <= 640
            return sm[:, so[0] - n:so[0]]

        ss_x, rstd, hrstd, rtmp = (small(NT) for _ in range(4))
        lss = v3(small(NT * 3), NT)
        lrs = v3(small(NT * 3), NT)
        ab = v3(small(NT * 2 * H), NT)
        a1, na, rl, lnp, g_, bt, beta, egc, edec, gdiff, begc = (v3(small(NT * H), NT) for _ in range(11))
        ea = small(H)
        gcs = v3(small(NT * 16), NT)
        eS = v3(small(NT * 2 * H), NT)
        ssd = [v3(small(NT * H), NT) for _ in range(2)]
        rq, rqg, rk, rkbg, rkd = (v3(small(NT * H), NT) for _ in range(5))
        oss = v3(small(NT * H), NT)
        ors = v3(small(NT * H), NT)
        hss = v3(small(NT * 12), NT)
        hrs = v3(small(NT * 12), NT)
        d_part = [hss[:, :, i * H:(i + 1) * H] for i in range(3)]
        d_root = [hrs[:, :, i * H:(i + 1) * H] for i in range(3)]
        mx, nmx, den = (small(4 * NT * H).rearrange("p (a t h) -> p a t h", a=4, t=NT) for _ in range(3))
        mr = v3(small(NT * H), NT)
        csum = v3(small(NT * H), NT)
        cmax = v3(small(NT * H), NT)
        cexp = small(GROUPS * NT * H).rearrange("p (a t h) -> p a t h", a=GROUPS, t=NT)
        cden = small(GROUPS * NT * H).rearrange("p (a t h) -> p a t h", a=GROUPS, t=NT)
        pos_i = small(NT).bitcast(I32)
        pos_f = small(NT)

        def const(name):
            a, n = TAB[name]
            return tab[:, a:a + n]

        def gains(name):
            a, n = GAIN[name]
            return gain[:, a:a + n]

        def d_slot(i):
            return 2 if i % 3 == 1 else i // 3 % 2

        ident = const("ident")

        def over_heads(ap):
            return ap.unsqueeze(1).broadcast_to([P, H, ap.shape[-1]])

        def per_head(ap, n=HD, h=H):
            return ap.unsqueeze(2).broadcast_to([P, h, n])

        ps = [ctx.enter_context(nc.psum_tensor(f"bank{b}", [P, 512], F32)) for b in range(8)]

        bank_full = [sem(f"bank_full{b}") for b in range(8)]
        bank_free = [sem(f"bank_free{b}") for b in range(8)]
        raw_loaded = [sem(f"raw_loaded{s}") for s in range(RAW)]
        start = {k: sem(k) for k in ("tab_first", "tab_loaded", "x_loaded0", "x_loaded1", "pos_loaded", "rows_loaded", "rows_T", "rows_copied",
                                     "angle_step", "angles", "sines", "rot_ready", "stored")}
        gains_loaded, hi_done, lo_done, half_done = (sem(k) for k in ("gains_loaded", "hi_done", "lo_done", "half_done"))
        z_tanh = [sem(f"z_tanh{t}") for t in range(NT)]
        own = {e: sem(f"{e}_own") for e in OWN}
        seen = dict.fromkeys(OWN, 0)
        part_done = {}

        OPEN = 1

        def full(step, layer, i=0):
            b = banks(step)[i]
            return bank_full[b], layer * TURNS[b] + OPEN + TURN[(step, b)] + 1

        def free(step, layer, i=0):
            b = banks(step)[i]
            return bank_free[b], layer * TURNS[b] + OPEN + TURN[(step, b)]

        def taken(step, layer, i=0):
            b = banks(step)[i]
            return bank_free[b], layer * TURNS[b] + OPEN + TURN[(step, b)] + 1

        def part(engine, step):
            key = f"{engine}_{step[0]}"
            if key not in part_done:
                part_done[key] = sem(key)
            return part_done[key]

        def after(engine, step, layer):
            return part(engine, step), layer * COUNT[step[0]] + PLACE[step] + 1

        def bank_unit(u):
            return ("unit", u - UNITS[u][2])

        def used(u, layer):
            if banks(("unit", u)) and not whole(u):
                return half_done, layer * HALVES + sum(bool(banks(("unit", v))) and not whole(v) for v in range(u)) + 1
            return full(bank_unit(u), layer, 1)

        def block_taken(u, layer):
            return taken(bank_unit(u), layer, 1)

        LAST = NU - 1

        def layer_start(layer):
            return bank_free[1], layer * TURNS[1] + OPEN

        def unit_of(what, i):
            return max(u for u in range(NU) if UNITS[u][:2] == (what, i))

        def view(buf, slot, nk, n):
            return buf[:, slot * 2048:slot * 2048 + nk * n].rearrange("p (c n) -> p c n", c=nk)

        def piece(nk, i):
            cut = (nk + 1) // 2
            return (0, cut) if i == 0 else (cut, nk)

        x_rows = x.rearrange("b (t p) d -> (b p) t d", p=P)
        out_rows = out.rearrange("b (t p) d -> (b p) t d", p=P)
        win = w_in.rearrange("l (c p) n -> l p c n", p=P)
        wqb = mla_w_q_b.rearrange("l (c p) n -> l p c n", p=P)
        wkvb = mla_w_kv_b.rearrange("l (c p) n -> l p c n", p=P)
        wbr = w_branch.rearrange("l b (c p) n -> l b p c n", p=P)
        wout = w_out.rearrange("l (c p) n -> l p c n", p=P)

        def sources(u, layer):
            what, i, hf, nk, n = UNITS[u]
            rows = slice(hf * nk, (hf + 1) * nk)
            if what == "qb":
                return [(0, wqb[layer, :, :, i * n:(i + 1) * n])]
            if what == "kvb":
                return [(0, wkvb[layer, :, :, i * n:(i + 1) * n])]
            if what == "branch":
                return [(0, wbr[layer, i // 2, :, :, (i % 2) * n:(i % 2 + 1) * n])]
            if what == "out":
                return [(0, wout[layer, :, rows, i * n:(i + 1) * n])]
            if what == "latq":
                return [(0, win[layer, :, rows, COL["ab"]:COL["ab"] + 2 * H]),
                        (2 * H, win[layer, :, rows, COL["q_lat"]:COL["q_lat"] + Q_RANK])]
            c = {"latkv": lambda: COL["kv_lat"], "dn": lambda: COL["dn"] + i * W, "z": lambda: COL[f"z{i}"],
                 "gate": lambda: COL["gate"] + i * 512,
                 "dil": lambda: COL["dil"] + (i % 3) * GROUPS * W + (i // 3) * W}[what]()
            return [(0, win[layer, :, rows, c:c + n])]

        block = ctx.enter_context(nc.Block())

        @block.sync
        def _(sp):
            for s in (*bank_free, *bank_full, lo_done):
                sp.sem_inc(s, OPEN)
            for r0, src in ((0, dn_conv_w.rearrange("l j (f p) -> (j f) l p", p=P)), (PRM_NORM, norm_g.rearrange("l (c p) -> c l p", p=P)),
                            (PRM_LAT, mla_q_a_norm_g.rearrange("l (c p) -> c l p", p=P)),
                            (PRM_LAT + Q_RANK // P, mla_kv_a_norm_g.rearrange("l (c p) -> c l p", p=P))):
                sp.dma_start(v3(prm_rows[r0:r0 + src.shape[0], :], DEPTH), src).then_inc(start["rows_loaded"], 16)
            for i in range(2):
                c = slice(i * D // 2, (i + 1) * D // 2)
                sp.dma_start(xs[:, :, c], x_rows[:, :, c]).then_inc(start[f"x_loaded{i}"], 16)
            with sp.Fori(0, DEPTH) as layer:
                for u in range(NU):
                    what, i, hf, nk, n = UNITS[u]
                    if u < RAW:
                        sp.wait_ge(lo_done, layer * (PIECES * NU) + OPEN)
                    else:
                        sp.wait_ge(lo_done, layer * (PIECES * NU) + OPEN + PIECES * (u - RAW + 1))
                    dst = view(raw, u % RAW, nk, n)
                    for c, src in sources(u, layer):
                        sp.dma_start(dst[:, :, c:c + src.shape[-1]], src).then_inc(raw_loaded[u % RAW], 16)
                    if u == RAW - 1:
                        sp.wait_ge(*layer_start(layer))
                        for name, src in (("mq", mla_q_norm_g), ("mk", mla_k_norm_g), ("dq", dil_q_norm_g), ("dk", dil_k_norm_g),
                                          ("dn", dn_out_norm_g), ("a_log", dn_a_log), ("dt", dn_dt_bias)):
                            v = src[layer]
                            sp.dma_start(gains(name), v.unsqueeze(0).broadcast_to([P, v.shape[0]])).then_inc(gains_loaded, 16)
            for i in range(2):
                c = slice(i * D // 2, (i + 1) * D // 2)
                sp.wait_ge(bank_free[1], DEPTH * TURNS[1] + OPEN - 1 + i)
                sp.dma_start(out_rows[:, :, c], xs[:, :, c]).then_inc(start["stored"], 16)
            sp.wait_ge(start["stored"], 2 * 16)

        @block.tensor
        def _(pe):
            mm, tr = nc.tensor.matmul, nc.tensor.transpose

            def unit(step, layer):
                u = step[1]
                what, i, hf, nk, n = UNITS[u]
                hi, lo = view(w_hi, u % SPLIT, nk, n), view(w_lo, u % SPLIT, nk, n)
                starts, ends = whole(u) or hf == 0, whole(u) or hf == 1
                src, k0 = (yT, 3 if what == "kvb" else 0) if whole(u) else (hT, hf * nk)
                if what == "qb":
                    pe.wait_ge(*taken(("latT", 2), layer))
                if what == "branch":
                    pe.wait_ge(*taken(("yT", i // 2, 1), layer))
                pair = "xT" if u < 2 else "mT" if what == "out" and i == 0 else None
                for t in range(NT):
                    if starts:
                        pe.wait_ge(*free(step, layer, t))
                    tok = slice(t * P, (t + 1) * P)
                    o = ps[t][:, 0:n]
                    for k in range(nk):
                        if t == 0 and pair and k % 2 == 0:
                            pe.wait_ge(*taken((pair, (k0 + k) // 2), layer))
                        if t == 0 and k in (0, piece(nk, 1)[0]):
                            pe.wait_ge(lo_done, layer * (PIECES * NU) + OPEN + PIECES * u + 1 + (k > 0))
                        mm(o, src[0][:, k0 + k, tok], hi[:, k, :], start=starts and k == 0, stop=False)
                        mm(o, src[0][:, k0 + k, tok], lo[:, k, :], start=False, stop=False)
                        last = mm(o, src[1][:, k0 + k, tok], hi[:, k, :], start=False, stop=ends and k == nk - 1)
                    if ends:
                        last.then_inc(bank_full[t], 1)
                if not ends:
                    last.then_inc(half_done, 1)

            def four(step, layer, product, i=0):
                pe.wait_ge(*free(step, layer, i))
                b = banks(step)[i]
                for h in range(H):
                    last = product(ps[b][:, h * P:(h + 1) * P], h)
                last.then_inc(bank_full[b], 1)

            def wait_taken(step, layer, *made):
                latest = {}
                for s in made:
                    s, i = s if isinstance(s[0], tuple) else (s, 0)
                    b = banks(s)[i]
                    latest[b] = max(latest.get(b, 0), TURN[(s, b)] + 1)
                for b, k in latest.items():
                    if b not in banks(step)[:1]:
                        pe.wait_ge(bank_free[b], layer * TURNS[b] + OPEN + k)

            def square(src, jp):
                return lambda o, j: tr(o, src[:, j % 2, (2 * jp + j // 2) * P:(2 * jp + j // 2 + 1) * P], ident)

            def hd(buf, t, h):
                return buf[:, t, h * P:(h + 1) * P]

            def xT(step, layer):
                if step[1] == 0:
                    pe.wait_ge(*layer_start(layer))
                pe.wait_ge(start[f"x_loaded{step[1] // 2}"], 16)
                four(step, layer, square(xs, step[1]))

            def mT(step, layer):
                if step[1] % 2 == 0:
                    pe.wait_ge(*after("gpsimd", evict_step(unit_of("branch", 2 * B + step[1] // 2)), layer))
                four(step, layer, square(mixed, step[1]))

            def yT_step(step, layer):
                _, n, jp = step
                pe.wait_ge(*after("vector", {A: ("m_out",), B: ("b_out",), C: ("d_out",)}[n], layer))
                four(step, layer, square(z, jp))

            def latT(step, layer):
                j = step[1]
                pe.wait_ge(*block_taken(3, layer))
                pe.wait_ge(*free(step, layer))
                b = banks(step)[0]
                for c in range(2 * j, min(2 * j + 2, 5)):
                    for t in range(NT):
                        last = tr(ps[b][:, (c % 2) * S + t * P:(c % 2) * S + (t + 1) * P], lat[:, t, c * P:(c + 1) * P], ident)
                last.then_inc(bank_full[b], 1)

            def tr_step(step, layer):
                _, what, i = step
                t = i % 2
                if what == "mkp":
                    pe.wait_ge(*after("gpsimd", ("kpe",), layer))
                    pe.wait_ge(*free(step, layer))
                    for tt in range(NT):
                        last = tr(ps[7][:, tt * P:(tt + 1) * P], lat[:, tt, Q_RANK + KV_RANK + ROPE - P:], ident)
                    last.then_inc(bank_full[7], 1)
                    return
                if what in ("q", "qg", "k"):
                    wait_taken(step, layer, ("dn_bT", int(what == "k"), t))
                else:
                    pe.wait_ge(*{
                             "mqn": lambda: after("vector", ("q_rope", t), layer), "mqp": lambda: after("gpsimd", ("q_rope", t), layer),
                             "mkn": lambda: after("vector", ("k_rs",), layer),
                             "dq": lambda: after("gpsimd", ("d_rope", i // 2, 0), layer),
                             "dk": lambda: after("gpsimd", ("d_rope", i // 2, 1), layer)}[what]())
                src = {"q": lambda h: hd(qn, t, h), "qg": lambda h: hd(qg, t, h), "k": lambda h: hd(kn, t, h),
                       "mqn": lambda h: mq[:, t, h * QK:h * QK + HD], "mqp": lambda h: mq[:, t, (h + 1) * QK - P:(h + 1) * QK],
                       "mkn": lambda h: kv[:, t, h * 2 * HD:h * 2 * HD + HD],
                       "dq": lambda h: hd(gate, t, h), "dk": lambda h: hd(gate, t, h)}[what]
                four(step, layer, lambda o, h: tr(o, src(h), ident))

            def sc(step, layer):
                _, a, t, j = step
                nk = (t + 1) * P
                if t == 0:
                    wait_taken(step, layer, *((("tr", "mkn", 1), ("tr", "mkp", 0)) if a == "m" else (("tr", "dk", 2 * a + 1),)))
                pe.wait_ge(*free(step, layer))
                b = banks(step)[0]
                tok = slice(t * P, (t + 1) * P)
                for n, h in enumerate(range(H) if t == 0 else (2 * j, 2 * j + 1)):
                    o = ps[b][:, n * nk:(n + 1) * nk]
                    if a == "m":
                        mm(o, mqnT[:, h, tok], mknT[:, h, 0:nk], start=True, stop=False)
                        last = mm(o, mqpT[P - ROPE:, h, tok], mkpT[P - ROPE:, 0:nk], start=False, stop=True)
                    else:
                        last = mm(o, dqT[:, h, tok], dkT[:, h, 0:nk], start=True, stop=True)
                last.then_inc(bank_full[b], 1)

            def pT(step, layer):
                _, a, t, j = step
                pe.wait_ge(*after("scalar", ("soft", a, t), layer))

                def one(o, n):
                    h, k = (n, 0) if t == 0 else (2 * j + n // 2, n % 2)
                    return tr(o, Sc[t][:, h, k * P:(k + 1) * P], ident)

                four(step, layer, one)

            def pv(step, layer):
                _, a, t, j = step
                pe.wait_ge(*taken(("pT", a, t, j), layer))
                pe.wait_ge(*block_taken(unit_of("kvb", 1) if a == "m" else unit_of("dil", 3 * a + 2), layer))
                if j == 0:
                    pe.wait_ge(*free(step, layer))
                pt = PT[:, PLACE[("pT", a, t, j)] % 2, :]

                def value(h, kt):
                    return kv[:, kt, h * 2 * HD + HD:(h + 1) * 2 * HD] if a == "m" else hd(dv, kt, h)

                for h in (range(H) if t == 0 else (2 * j, 2 * j + 1)):
                    for kt in range(t + 1):
                        c = (h if t == 0 else h % 2 * 2 + kt) * P
                        last = mm(ps[4][:, h * P:(h + 1) * P], pt[:, c:c + P], value(h, kt), start=kt == 0, stop=kt == t)
                if j == t:
                    last.then_inc(bank_full[4], 1)

            def dn_gc(step, layer):
                pe.wait_ge(*after("vector", ("dn_g1",), layer))
                pe.wait_ge(start["tab_loaded"], 16)
                pe.wait_ge(*free(step, layer))
                for t in range(NT):
                    for i, w in enumerate((const("tri"), const("same"), const("chunk")[:, 0:1].broadcast_to([P, P]),
                                           const("chunk")[:, 1:2].broadcast_to([P, P]))):
                        last = mm(ps[3][:, (t * 4 + i) * H:(t * 4 + i + 1) * H], w, g_[:, t, :], start=True, stop=True)
                last.then_inc(bank_full[3], 1)

            def dn_row(step, layer):
                t = step[1]
                four(step, layer, lambda o, h: mm(o, g_[:, t, h:h + 1].broadcast_to([P, P]), const("tri"), start=True, stop=True))

            def dn_fT(step, layer):
                _, i, j = step
                pe.wait_ge(*block_taken(unit_of("dn", i), layer))
                four(step, layer, square(mix, j))

            def dn_ss(step, layer):
                pe.wait_ge(*after("scalar", ("dn_sq", step[1]), layer))
                pe.wait_ge(*free(step, layer))
                for t in range(NT):
                    for h in range(H):
                        last = mm(ps[3][:, t * H + h:t * H + h + 1], th_f[:, h, t * P:(t + 1) * P], const("one"), start=True, stop=True)
                last.then_inc(bank_full[3], 1)

            def dn_bT(step, layer):
                _, i, t = step
                pe.wait_ge(*after("vector", ("dn_silu", i), layer))
                four(step, layer, lambda o, h: tr(o, feat[:, h, t * P:(t + 1) * P], ident))

            def dn_kk(step, layer):
                t = step[1]
                wait_taken(step, layer, ("tr", "k", t))
                four(step, layer, lambda o, h: mm(o, hd(kT, t, h), hd(kT, t, h), start=True, stop=True))

            def dn_qk(step, layer):
                t = step[1]
                wait_taken(step, layer, ("tr", "q", t))
                four(step, layer, lambda o, h: mm(o, hd(kT, t, h), hd(qT, t, h), start=True, stop=True))

            def dn_U(step, layer):
                t = step[1]
                wait_taken(step, layer, ("dn_kk", t))
                four(step, layer, lambda o, h: tr(o, hd(L, t, h), ident))

            def dn_X(step, layer):
                _, s, t = step
                pe.wait_ge(*after("gpsimd", ("dn_M", s, t), layer))
                if s == 1:
                    pe.wait_ge(*after("gpsimd", ("dn_U", t), layer))
                    pe.wait_ge(*after("vector", ("dn_U", t), layer))
                else:
                    wait_taken(step, layer, (("dn_TX", s - 1, t), 0))
                four(step, layer, lambda o, h: mm(o, hd(d_Us, t, h), hd(d_T, t, h), start=True, stop=True))

            def dn_TX(step, layer):
                _, s, t = step
                wait_taken(step, layer, ("dn_X", s, t), *([(("dn_TX", s - 1, t), 1)] if s > 1 else []))
                final = s == len(LEVELS) - 1
                if not final:
                    four(step, layer, lambda o, h: mm(o, hd(d_TT, t, h), hd(X, t, h), start=True, stop=True), 0)
                four(step, layer, lambda o, h: mm(o, hd(X, t, h), hd(d_TT, t, h), start=True, stop=True), 0 if final else 1)

            def dn_u(step, layer):
                t = step[1]
                wait_taken(step, layer, ("dn_TX", len(LEVELS) - 1, t), ("dn_bT", 2, t))
                four(step, layer, lambda o, h: mm(o, hd(d_TT, t, h), hd(vb, t, h), start=True, stop=True))

            def dn_w(step, layer):
                t = step[1]
                four(step, layer, lambda o, h: mm(o, hd(kbg, t, h), hd(d_TT, t, h), start=True, stop=True))

            def dn_ds(step, layer):
                c = step[1]
                t, r = c // 2, slice(CH * (c % 2), CH * (c % 2) + CH)
                if c == 0:
                    pe.wait_ge(*after("vector", ("dn_v0",), layer))
                else:
                    wait_taken(step, layer, ("dn_ws", c))
                four(step, layer, lambda o, h: mm(o, hd(kdec, t, h)[r, :], hd(vnew, t, h)[r, :], start=True, stop=True))

            def dn_ws(step, layer):
                c = step[1]
                t, r = c // 2, slice(CH * (c % 2), CH * (c % 2) + CH)
                wait_taken(step, layer, ("dn_w", t), ("dn_ds", c - 1))
                four(step, layer, lambda o, h: mm(o[r, :], hd(wT, t, h)[:, r], states[c][:, h * P:(h + 1) * P], start=True, stop=True))

            def dn_o(step, layer):
                t = step[1]
                wait_taken(step, layer, ("dn_ws", 2 * t + 1), ("tr", "qg", t), ("dn_qk", t))

                def one(o, h):
                    mm(o, hd(Aqk, t, h), hd(vnew, t, h), start=True, stop=False, skip_group_check=True)
                    for c in (2 * t, 2 * t + 1):
                        if c > 0:
                            r = slice(CH * (c % 2), CH * (c % 2) + CH)
                            last = mm(o[r, :], hd(qgT, t, h)[:, r], states[c][:, h * P:(h + 1) * P], start=False, stop=True,
                                      skip_group_check=True)
                    return last

                four(step, layer, one)

            parts = {"unit": unit, "xT": xT, "mT": mT, "yT": yT_step, "latT": latT, "tr": tr_step, "sc": sc, "pT": pT, "pv": pv,
                     "dn_gc": dn_gc, "dn_row": dn_row, "dn_fT": dn_fT, "dn_ss": dn_ss, "dn_bT": dn_bT, "dn_kk": dn_kk,
                     "dn_qk": dn_qk, "dn_U": dn_U, "dn_X": dn_X, "dn_TX": dn_TX, "dn_u": dn_u, "dn_w": dn_w, "dn_ds": dn_ds,
                     "dn_ws": dn_ws, "dn_o": dn_o}
            pe.wait_ge(start["tab_first"], 16)
            pe.wait_ge(start["rows_loaded"], 64)
            for d in range(DEPTH):
                last = tr(ps[7][:, d * PRM_ROWS:(d + 1) * PRM_ROWS], prm_rows[:, d * P:(d + 1) * P], ident[0:PRM_ROWS, 0:PRM_ROWS])
            last.then_inc(start["rows_T"], 1)
            pe.wait_ge(start["rows_copied"], 1)
            with pe.Fori(0, DEPTH) as layer:
                for step in ORDER:
                    if step[0] in parts:
                        parts[step[0]](step, layer)

        @block.scalar
        def _(act):
            av = nc.scalar.activation

            def own_next(ins, layer):
                seen["scalar"] += 1
                ins.then_inc(own["scalar"], 1)
                act.wait_ge(own["scalar"], layer * OWN["scalar"] + seen["scalar"])

            def prep(step, layer):
                u = step[1]
                what, i, hf, nk, n = UNITS[u]
                act.wait_ge(raw_loaded[u % RAW], layer * (16 * RAW_TOTAL[u % RAW]) + 16 * RAW_AT[u])
                act.wait_ge(*(used(u - SPLIT, layer) if u >= SPLIT else (bank_full[1], layer * TURNS[1] + OPEN)))
                for p in range(PIECES):
                    a, b = piece(nk, p)
                    av(view(w_hi, u % SPLIT, nk, n)[:, a:b, :], view(raw, u % RAW, nk, n)[:, a:b, :], ACT.Copy).then_inc(hi_done, 1)

            def evict(step, layer):
                u = step[1]
                what, i, hf, nk, n = UNITS[u]
                key = bank_unit(u)
                if what == "out":
                    return
                if what == "latq":
                    act.wait_ge(*after("gpsimd", ("norm",), layer))
                elif what == "dn" and i > 0:
                    act.wait_ge(*full(("dn_fT", i - 1, 1), layer))
                elif what in ("qb", "kvb") and i == 0:
                    act.wait_ge(*after("gpsimd", ("lat_norm",), layer))
                elif what == "dil" and i % 3 < 2:
                    if i == 0:
                        act.wait_ge(*full(("tr", "mkp", 0), layer))
                    else:
                        act.wait_ge(*after("gpsimd", ("d_rope", (i - 1) // 3, 0) if i % 3 == 1 else ("d_rope", i // 3 - 1, 1), layer))
                elif what == "z" and i != A:
                    act.wait_ge(*full(("yT", {C: A, B: C}[i], 1), layer))
                elif what == "gate":
                    if i == GATES[0]:
                        for e in ("gpsimd", "vector"):
                            act.wait_ge(*after(e, ("q_rope", 1), layer))
                        act.wait_ge(*after("gpsimd", ("kpe",), layer))
                    else:
                        b = unit_of("branch", GATES[GATES.index(i) - 1])
                        act.wait_ge(*(block_taken(b, layer) if UNITS[b][1] // 2 == A else after("gpsimd", evict_step(b), layer)))
                    if i == GATES[1]:
                        act.wait_ge(*full(("tr", "dk", 2 * GROUPS - 1), layer))
                for t in range(NT):
                    if what == "dil" and i % 3 == 2 and t == 0:
                        if i > 2:
                            act.wait_ge(*full(("pv", i // 3 - 1, 1, 0), layer))
                        else:
                            act.wait_ge(*full(("pv", "m", 1, 0), layer))
                            act.wait_ge(*after("vector", ("m_out",), layer))
                    act.wait_ge(*full(key, layer, t))
                    o = ps[t][:, 0:n]
                    if what == "latq":
                        av(ab[:, t, :], o[:, 0:2 * H], ACT.Copy, scale=rstd[:, t:t + 1])
                        dst, o, func, scale = lat[:, t, 0:Q_RANK], o[:, 2 * H:n], ACT.Copy, rstd[:, t:t + 1]
                    elif what == "latkv":
                        dst, func, scale = lat[:, t, Q_RANK:], ACT.Copy, rstd[:, t:t + 1]
                    elif what == "dn":
                        dst, func, scale = mix[:, t, :], ACT.Copy, rstd[:, t:t + 1]
                    elif what == "qb":
                        dst, func, scale = mq[:, t, i * n:(i + 1) * n], ACT.Copy, lrs[:, t, 0:1]
                    elif what == "kvb":
                        dst, func, scale = kv[:, t, i * n:(i + 1) * n], ACT.Copy, lrs[:, t, 1:2]
                    elif what == "dil":
                        dst, func, scale = (stg if i % 3 < 2 else dv)[:, t, :], ACT.Copy, rstd[:, t:t + 1]
                    elif what == "z":
                        dst, func, scale = z[:, t, :], ACT.Tanh, hrstd[:, t:t + 1]
                    elif what == "gate":
                        dst, func, scale = gate[:, t, :], ACT.Tanh, hrstd[:, t:t + 1]
                    if what == "dil" and i % 3 < 2:
                        if t == 0 and i > 2:
                            act.wait_ge(*after("gpsimd", ("d_rs", i // 3 - 1, i % 3), layer))
                        for h in range(H):
                            c = slice(h * HD, (h + 1) * HD)
                            ins = av(dst[:, c], o[:, c], ACT.Square, scale=scale, accum_out=d_part[d_slot(i)][:, t, h:h + 1])
                        own_next(ins, layer)
                    if what == "qb":
                        for h in range(2):
                            for c, n_, j in ((h * QK, HD, 2 * i + h), (h * QK + HD, ROPE, H + 2 * i + h)):
                                ins = av(dst[:, c:c + n_], o[:, c:c + n_], ACT.Square, scale=scale, accum_out=hss[:, t, j:j + 1])
                        own_next(ins, layer)
                    if what == "kvb":
                        for h in range(2):
                            c, j = h * 2 * HD, 2 * H + 2 * i + h
                            ins = av(dst[:, c:c + HD], o[:, c:c + HD], ACT.Square, scale=scale, accum_out=hss[:, t, j:j + 1])
                        own_next(ins, layer)
                    ins = av(dst, o, func, scale=scale)
                    ins.then_inc(z_tanh[t] if what == "z" else bank_free[t], 1)

            def norm(step, layer):
                for i in range(2):
                    act.wait_ge(start[f"x_loaded{i}"], 16)
                act.wait_ge(start["rot_ready"], 1)
                act.wait_ge(*layer_start(layer))
                for t in range(NT):
                    last = av(mixed[:, t, :], xs[:, t, :], ACT.Square, accum_out=ss_x[:, t:t + 1])
                last.then_inc(part("scalar", step), 1)

            def load(step, layer):
                act.wait_ge(start["rows_copied"], 1)
                act.wait_ge(*layer_start(layer))
                av(prm[:, 0:ROWS_CONV], prm_all[:, bass.ds(layer * PRM_ROWS, ROWS_CONV)], ACT.Copy, scale=0.5)
                av(prm[:, ROWS_CONV:], prm_all[:, bass.ds(layer * PRM_ROWS + ROWS_CONV, PRM_ROWS - ROWS_CONV)], ACT.Copy)\
                    .then_inc(part("scalar", step), 1)

            def split_hi(step, layer, k0, dst, scale, n=2):
                act.wait_ge(*full(step, layer))
                for j in range(n):
                    last = av(dst[0][:, k0 + j, :], ps[banks(step)[0]][:, j * S:(j + 1) * S], ACT.Copy, scale=scale(k0 + j))
                last.then_inc(part("scalar", step), 1)

            def xT(step, layer):
                if step[1] == 0:
                    act.wait_ge(*after("scalar", ("load",), layer))
                split_hi(step, layer, 2 * step[1], hT, lambda c: prm[:, PRM_NORM + c:PRM_NORM + c + 1])

            def mT(step, layer):
                split_hi(step, layer, 2 * step[1], hT, lambda c: 0.5)

            def latT(step, layer):
                j = step[1]
                split_hi(step, layer, 2 * j, yT, lambda c: prm[:, PRM_LAT + c:PRM_LAT + c + 1], 2 if j < 2 else 1)

            def yT_step(step, layer):
                _, n, j = step
                act.wait_ge(*used({A: unit_of("kvb", 1), C: unit_of("branch", 2 * A + 1), B: unit_of("branch", 2 * C + 1)}[n], layer))
                split_hi(step, layer, 2 * j, yT, lambda c: 1.0)

            def lat_norm(step, layer):
                act.wait_ge(*block_taken(3, layer))
                junk = at[:, 0:NT * 704]
                for t in range(NT):
                    for i, (a, b) in enumerate(((0, Q_RANK), (Q_RANK, Q_RANK + KV_RANK), (Q_RANK + KV_RANK, 704))):
                        last = av(junk[:, t * 704 + a:t * 704 + b], lat[:, t, a:b], ACT.Square, accum_out=lss[:, t, i:i + 1])
                last.then_inc(part("scalar", step), 1)

            def dn_g0(step, layer):
                act.wait_ge(*after("vector", step, layer))
                av(ea, gains("a_log"), ACT.Exp)
                av(bt, ab[:, :, H:2 * H], ACT.Tanh, scale=0.5)
                own_next(av(na, na, ACT.Exp), layer)
                av(lnp, na, ACT.Ln, bias=1.0).then_inc(part("scalar", step), 1)

            def dn_gc(step, layer):
                act.wait_ge(*after("vector", step, layer))
                av(egc, gcs[:, :, 0:H], ACT.Exp)
                av(eS, gcs[:, :, 2 * H:4 * H], ACT.Exp)
                av(edec, gdiff, ACT.Exp).then_inc(part("scalar", step), 1)

            def dn_decay(step, layer):
                t = step[1]
                act.wait_ge(*after("vector", ("dn_row", t), layer))
                av(d_D[:, t, :], d_D[:, t, :], ACT.Exp, scale=-1.0)
                av(d_Dt[:, t, :], d_Dt[:, t, :], ACT.Exp).then_inc(part("scalar", step), 1)

            def dn_th(step, layer):
                act.wait_ge(*taken(("dn_fT", step[1], 1), layer))
                av(th, conv, ACT.Tanh).then_inc(part("scalar", step), 1)

            def dn_sq(step, layer):
                act.wait_ge(*after("vector", ("dn_silu", step[1]), layer))
                av(th, conv, ACT.Square).then_inc(part("scalar", step), 1)

            def copies(step, layer):
                k, *a = step
                b = banks(step)[0]
                src = ps[b][:, :]
                t = a[-1] % 2
                tok = slice(t * P, (t + 1) * P)
                act.wait_ge(*full(step, layer))
                if k == "tr":
                    what = a[0]
                    if what == "mkp":
                        act.copy(mkpT[P - ROPE:, :], src[P - ROPE:, 0:S]).then_inc(bank_free[b], 1)
                        return
                    if what in ("q", "qg", "k"):
                        dst = {"q": qT, "qg": qgT, "k": kT}[what][:, t, :]
                    else:
                        r0 = P - ROPE if what == "mqp" else 0
                        dst = {"mqn": mqnT, "mqp": mqpT, "mkn": mknT, "dq": dqT, "dk": dkT}[what][r0:, :, tok]
                        src = heads(src[r0:, :])
                elif k == "pT":
                    dst = PT[:, PLACE[step] % 2, :]
                elif k == "pv":
                    if a[1] != a[2]:
                        return
                    dst = og[a[0]][:, a[1], :]
                else:
                    dst = {"dn_U": d_U, "dn_X": X, "dn_u": u_, "dn_w": wT, "dn_o": o_sb}[k][:, t, :]
                act.copy(dst, src).then_inc(bank_free[b], 1)

            def pv(step, layer):
                if step[1] != "m" and step[2] == step[3]:
                    b = 4
                    act.wait_ge(*full(("pv", step[1], step[2], 0), layer))
                    act.copy(og[step[1]][:, step[2], :], ps[b][:, :]).then_inc(bank_free[b], 1)

            def soft(step, layer):
                _, a, t = step
                n = 0 if a == "m" else 1 + a
                act.wait_ge(*after("vector", step, layer))
                for h in range(H):
                    s = Sc[t][:, h, :]
                    scale = QK ** -0.5 if a == "m" else d_root[d_slot(3 * a)][:, t, h:h + 1]
                    last = av(s, s, ACT.Exp, bias=nmx[:, n, t, h:h + 1], scale=scale, accum_out=den[:, n, t, h:h + 1])
                last.then_inc(part("scalar", step), 1)

            def d_c0(step, layer):
                act.wait_ge(*after("vector", step, layer))
                av(cexp, cexp, ACT.Exp).then_inc(part("scalar", step), 1)

            parts = {"prep": prep, "evict": evict, "evict_z": evict, "norm": norm, "load": load, "xT": xT, "mT": mT, "latT": latT, "yT": yT_step, "lat_norm": lat_norm,
                     "dn_g0": dn_g0, "dn_gc": dn_gc, "dn_decay": dn_decay, "dn_th": dn_th, "dn_sq": dn_sq, "pv": pv, "soft": soft, "d_c0": d_c0,
                     **dict.fromkeys(("tr", "pT", "dn_U", "dn_X", "dn_u", "dn_w", "dn_o"), copies)}
            act.dma_start(tab[:, 0:TAB_FIRST], tables[:, 0:TAB_FIRST]).then_inc(start["tab_first"], 16)
            act.dma_start(pos_i[:, :], positions.rearrange("b (t p) -> (b p) t", p=P), allow_slow_non_contiguous=True).then_inc(start["pos_loaded"], 16)
            act.wait_ge(start["angles"], 1)
            av(mixed[:, 0, 0:384], mixed[:, 0, 0:384], ACT.Sin).then_inc(start["sines"], 1)
            act.dma_start(tab[:, TAB_FIRST:], tables[:, TAB_FIRST:]).then_inc(start["tab_loaded"], 16)
            act.wait_ge(start["tab_first"], 16)
            av(ea[:, 0:1], const("one"), ACT.Exp)
            with act.Fori(0, DEPTH) as layer:
                for step in ORDER:
                    if step[0] in parts:
                        parts[step[0]](step, layer)

        @block.vector
        def _(dve):
            tt, ts, stt = nc.vector.tensor_tensor, nc.vector.tensor_scalar, nc.vector.scalar_tensor_tensor

            def own_next(ins, layer):
                seen["vector"] += 1
                ins.then_inc(own["vector"], 1)
                dve.wait_ge(own["vector"], layer * OWN["vector"] + seen["vector"])

            def prep(step, layer):
                u = step[1]
                what, i, hf, nk, n = UNITS[u]
                for p in range(PIECES):
                    a, b = piece(nk, p)
                    dve.wait_ge(hi_done, layer * (PIECES * NU) + PIECES * u + p + 1)
                    tt(view(w_lo, u % SPLIT, nk, n)[:, a:b, :], view(raw, u % RAW, nk, n)[:, a:b, :],
                       view(w_hi, u % SPLIT, nk, n)[:, a:b, :].bitcast(F32), ALU.subtract).then_inc(lo_done, 1)

            def evict(step, layer):
                u = step[1]
                what, i, hf, nk, n = UNITS[u]
                key = bank_unit(u)
                if what == "z":
                    for t in range(NT):
                        dve.wait_ge(z_tanh[t], layer * BRANCHES + (A, C, B).index(i) + 1)
                        stt(z[:, t, :], z[:, t, :], 1.0, ps[t][:, 0:n], ALU.add, ALU.mult).then_inc(bank_free[t], 1)
                elif what == "branch":
                    dve.wait_ge(*block_taken(unit_of("gate", i), layer))
                    if i // 2 == A and i % 2 == 0:
                        dve.wait_ge(*after("scalar", ("norm",), layer))
                    for t in range(NT):
                        dve.wait_ge(*full(key, layer, t))
                        dst = mixed[:, t, (i % 2) * n:(i % 2 + 1) * n] if i // 2 == A else gate[:, t, :]
                        stt(dst, gate[:, t, :], 1.0, ps[t][:, 0:n], ALU.add, ALU.mult).then_inc(bank_free[t], 1)
                elif what == "out":
                    for t in range(NT):
                        dve.wait_ge(*full(key, layer, t))
                        c = slice(i * n, (i + 1) * n)
                        tt(xs[:, t, c], xs[:, t, c], ps[t][:, 0:n], ALU.add).then_inc(bank_free[t], 1)

            def split_lo(step, layer, k0, dst, scale, n=2):
                b = banks(step)[0]
                dve.wait_ge(*after("scalar", step, layer))
                for j in range(n):
                    last = stt(dst[1][:, k0 + j, :], ps[b][:, j * S:(j + 1) * S], scale(k0 + j), dst[0][:, k0 + j, :].bitcast(F32),
                               ALU.mult, ALU.subtract)
                last.then_inc(bank_free[b], 1)

            def xT(step, layer):
                split_lo(step, layer, 2 * step[1], hT, lambda c: prm[:, PRM_NORM + c:PRM_NORM + c + 1])

            def mT(step, layer):
                split_lo(step, layer, 2 * step[1], hT, lambda c: 0.5)

            def latT(step, layer):
                j = step[1]
                split_lo(step, layer, 2 * j, yT, lambda c: prm[:, PRM_LAT + c:PRM_LAT + c + 1], 2 if j < 2 else 1)

            def yT_step(step, layer):
                split_lo(step, layer, 2 * step[2], yT, lambda c: 1.0)

            def dn_g0(step, layer):
                dve.wait_ge(gains_loaded, layer * (7 * 16) + 7 * 16)
                dve.wait_ge(*block_taken(1, layer))
                own_next(tt(a1, ab[:, :, 0:H], gains("dt").unsqueeze(1).broadcast_to([P, NT, H]), ALU.add), layer)
                stt(na, a1, -1.0, a1, ALU.mult, ALU.min).then_inc(part("vector", step), 1)

            def dn_g1(step, layer):
                dve.wait_ge(*after("scalar", ("dn_g0",), layer))
                own_next(stt(rl, a1, 0.0, lnp, ALU.max, ALU.add), layer)
                ts(beta, bt, 0.5, 0.5, ALU.mult, ALU.add)
                stt(g_, rl, -1.0, ea.unsqueeze(1).broadcast_to([P, NT, H]), ALU.mult, ALU.mult).then_inc(part("vector", step), 1)

            def dn_gc(step, layer):
                dve.wait_ge(*full(step, layer))
                dve.wait_ge(start["tab_loaded"], 16)
                nc.vector.tensor_copy(gcs, ps[3][:, 0:NT * 16].rearrange("p (t n) -> p t n", t=NT)).then_inc(bank_free[3], 1)
                dve.wait_ge(*taken(step, layer))
                tt(gdiff, gcs[:, :, H:2 * H], gcs[:, :, 0:H], ALU.subtract).then_inc(part("vector", step), 1)

            def dn_row(step, layer):
                t = step[1]
                b = banks(step)[0]
                dve.wait_ge(*full(step, layer))
                tt(heads(d_D[:, t, :]), heads(ps[b][:, :]), per_head(gcs[:, t, 0:H]), ALU.subtract).then_inc(bank_free[b], 1)
                dve.wait_ge(*taken(step, layer))
                own_next(ts(d_Dt[:, t, :], d_D[:, t, :], 0.0, None, ALU.min), layer)
                ts(d_D[:, t, :], d_D[:, t, :], 0.0, None, ALU.max).then_inc(part("vector", step), 1)

            def dn_fT(step, layer):
                _, i, j = step
                b = banks(step)[0]
                dve.wait_ge(*full(step, layer))

                def tap(k, n):
                    c = (CONV - 1 - k) * (3 * H) + i * H + 2 * j + n
                    return prm[:, c:c + 1]

                for n in range(2):
                    ins = ts(feat[:, 2 * j + n, :], ps[b][:, n * S:(n + 1) * S], tap(0, n), None, ALU.mult)
                own_next(ins, layer)
                for k in range(1, CONV):
                    for n in range(2):
                        y = feat[:, 2 * j + n, k:S]
                        ins = stt(y, ps[b][:, n * S:(n + 1) * S - k], tap(k, n), y, ALU.mult, ALU.add)
                    if k < CONV - 1:
                        own_next(ins, layer)
                ins.then_inc(bank_free[b], 1)

            def dn_silu(step, layer):
                i = step[1]
                dve.wait_ge(*after("scalar", ("dn_th", i), layer))
                stt(conv, th, 1.0, conv, ALU.add, ALU.mult).then_inc(part("vector", step), 1)

            def dn_ss(step, layer):
                i = step[1]
                dve.wait_ge(*full(step, layer))
                ts(ssd[i], ps[3][:, 0:NT * H].rearrange("p (t n) -> p t n", t=NT), 1e-6, None, ALU.add).then_inc(bank_free[3], 1)

            def dn_bT(step, layer):
                _, i, t = step
                b = banks(step)[0]
                if i < 2 and t == 0:
                    dve.wait_ge(*after("gpsimd", ("dn_ss", i), layer))
                if i == 1 and t == 0:
                    dve.wait_ge(*full(("tr", "qg", 1), layer))
                dve.wait_ge(*full(step, layer))
                o = heads(ps[b][:, :])
                for dst, f in (((qn, rq), (qg, rqg)), ((kn, rk), (kbg, rkbg), (kdec, rkd)), ((vb, beta),))[i]:
                    last = tt(heads(dst[:, t, :]), o, per_head(f[:, t, :]), ALU.mult)
                last.then_inc(bank_free[b], 1)

            def dn_kk(step, layer):
                t = step[1]
                b = banks(step)[0]
                dve.wait_ge(*after("gpsimd", ("dn_decay", t), layer))
                dve.wait_ge(*full(step, layer))
                tt(L[:, t, :], ps[b][:, :], d_D[:, t, :], ALU.mult).then_inc(bank_free[b], 1)

            def dn_qk(step, layer):
                t = step[1]
                b = banks(step)[0]
                dve.wait_ge(*full(step, layer))
                tt(Aqk[:, t, :], ps[b][:, :], d_Dt[:, t, :], ALU.mult).then_inc(bank_free[b], 1)

            def dn_U(step, layer):
                t = step[1]
                dve.wait_ge(*full(step, layer))
                own_next(tt(heads(d_T[:, t, :]), heads(L[:, t, :]), over_heads(const("level")), ALU.mult), layer)
                tt(heads(d_T[:, t, :]), over_heads(ident), heads(d_T[:, t, :]), ALU.subtract).then_inc(part("vector", step), 1)

            def dn_TX(step, layer):
                _, s, t = step
                final = s == len(LEVELS) - 1
                for i, dst in enumerate((d_TT,) if final else (d_T, d_TT)):
                    b = banks(step)[i]
                    dve.wait_ge(*full(step, layer, i))
                    tt(dst[:, t, :], dst[:, t, :], ps[b][:, :], ALU.subtract).then_inc(bank_free[b], 1)

            def dn_v0(step, layer):
                dve.wait_ge(*taken(("dn_u", 0), layer))
                nc.vector.tensor_copy(vnew[0:CH, 0, :], u_[0:CH, 0, :]).then_inc(part("vector", step), 1)

            def dn_ws(step, layer):
                c = step[1]
                t, r = c // 2, slice(CH * (c % 2), CH * (c % 2) + CH)
                b = banks(step)[0]
                dve.wait_ge(*full(step, layer))
                tt(vnew[r, t, :], u_[r, t, :], ps[b][r, :], ALU.subtract).then_inc(bank_free[b], 1)

            def dn_ds(step, layer):
                c = step[1]
                b = banks(step)[0]
                dve.wait_ge(*full(step, layer))
                if c == 0:
                    nc.vector.tensor_copy(states[1], ps[b][:, :]).then_inc(bank_free[b], 1)
                else:
                    dve.wait_ge(*after("gpsimd", ("dn_dec", c), layer))
                    tt(states[c + 1], states[c + 1], ps[b][:, :], ALU.add).then_inc(bank_free[b], 1)

            def dn_o(step, layer):
                t = step[1]
                dve.wait_ge(*after("gpsimd", step, layer))
                nc.vector.tensor_reduce(oss[:, t, :], heads(o_sq[:, t, :]), AX.X, ALU.add).then_inc(part("vector", step), 1)

            def b_out(step, layer):
                dve.wait_ge(*after("gpsimd", ("dn_on",), layer))
                dve.wait_ge(*block_taken(unit_of("z", B), layer))
                for t in range(NT):
                    last = tt(heads(o_sb[:, t, :]), heads(o_sb[:, t, :]), per_head(ors[:, t, :]), ALU.mult)
                own_next(last, layer)
                tt(z, z, o_sb, ALU.mult).then_inc(part("vector", step), 1)

            def q_rope(step, layer):
                t = step[1]
                dve.wait_ge(*after("gpsimd", ("q_rs",), layer))
                for h in range(H):
                    q = mq[:, t, h * QK:h * QK + HD]
                    last = stt(q, q, hrs[:, t, h:h + 1], gains("mq")[:, 0:HD], ALU.mult, ALU.mult)
                last.then_inc(part("vector", step), 1)

            def k_rs(step, layer):
                dve.wait_ge(*after("gpsimd", step, layer))
                for t in range(NT):
                    for h in range(H):
                        k = kv[:, t, h * 2 * HD:h * 2 * HD + HD]
                        last = stt(k, k, hrs[:, t, 2 * H + h:2 * H + h + 1], gains("mk")[:, 0:HD], ALU.mult, ALU.mult)
                last.then_inc(part("vector", step), 1)

            def sc(step, layer):
                _, a, t, j = step
                b = banks(step)[0]
                nk = (t + 1) * P
                m = const(f"mask_{a}")[:, (1 - t) * P:2 * P]
                hs = slice(0, H) if t == 0 else slice(2 * j, 2 * j + 2)
                n = hs.stop - hs.start
                dve.wait_ge(*full(step, layer))
                tt(Sc[t][:, hs, :], ps[b][:, :].rearrange("p (h k) -> p h k", k=nk), m.unsqueeze(1).broadcast_to([P, n, nk]), ALU.add)\
                    .then_inc(bank_free[b], 1)

            def soft(step, layer):
                _, a, t = step
                n = 0 if a == "m" else 1 + a
                dve.wait_ge(*taken(("sc", a, t, t), layer))
                own_next(nc.vector.tensor_reduce(mx[:, n, t, :], Sc[t], AX.X, ALU.max), layer)
                if a == "m":
                    ts(nmx[:, n, t, :], mx[:, n, t, :], -QK ** -0.5, None, ALU.mult).then_inc(part("vector", step), 1)
                else:
                    dve.wait_ge(*after("gpsimd", ("d_rs", a, 0), layer))
                    stt(nmx[:, n, t, :], mx[:, n, t, :], -1.0, d_root[d_slot(3 * a)][:, t, :], ALU.mult, ALU.mult)\
                        .then_inc(part("vector", step), 1)

            def pv(step, layer):
                _, a, t, j = step
                if a != "m" or j != t:
                    return
                dve.wait_ge(*after("scalar", ("soft", a, t), layer))
                own_next(nc.vector.reciprocal(mr[:, t, :], den[:, 0, t, :]), layer)
                own_next(ts(mr[:, t, :], mr[:, t, :], hrstd[:, t:t + 1], None, ALU.mult), layer)
                dve.wait_ge(*full(("pv", a, t, 0), layer))
                tt(heads(m_o[t]), heads(ps[4][:, :]), per_head(mr[:, t, :]), ALU.mult).then_inc(bank_free[4], 1)

            def m_out(step, layer):
                dve.wait_ge(*taken(("pv", "m", 1, 0), layer))
                dve.wait_ge(*block_taken(unit_of("z", A), layer))
                for t in range(NT):
                    last = tt(z[:, t, :], z[:, t, :], m_o[t], ALU.mult)
                last.then_inc(part("vector", step), 1)

            def d_rope(step, layer):
                _, g, k = step
                name = "dq" if k == 0 else "dk"
                if g == 0 and k == 0:
                    dve.wait_ge(*after("gpsimd", ("d_tables",), layer))
                else:
                    dve.wait_ge(*full(("tr", "dq", 2 * g + 1) if k else ("tr", "dk", 2 * g - 1), layer))
                dve.wait_ge(*block_taken(unit_of("dil", 3 * g + k) if g + k > 0 else unit_of("branch", GATES[0]), layer))
                s4 = stg.rearrange("p t (h d) -> p t h d", h=H)
                g4 = gate.rearrange("p t (h d) -> p t h d", h=H)
                tt(g4, s4, rg[name][0].unsqueeze(2).broadcast_to([P, NT, H, HD]), ALU.mult)
                tt(s4, s4, rg[name][1].unsqueeze(2).broadcast_to([P, NT, H, HD]), ALU.mult).then_inc(part("vector", step), 1)

            n3 = nmx.rearrange("p a t h -> p a (t h)")[:, 1:, :]
            d3 = den.rearrange("p a t h -> p a (t h)")[:, 1:, :]
            c3 = cexp.rearrange("p a t h -> p a (t h)")
            e3 = cden.rearrange("p a t h -> p a (t h)")

            def row(v):
                return v.rearrange("p t h -> p (t h)")

            def d_c0(step, layer):
                dve.wait_ge(*after("scalar", ("soft", 2, 1), layer))
                own_next(tt(row(cmax), n3[:, 0, :], n3[:, 1, :], ALU.min), layer)
                own_next(tt(row(cmax), row(cmax), n3[:, 2, :], ALU.min), layer)
                tt(c3, row(cmax).unsqueeze(1).broadcast_to([P, GROUPS, NT * H]), n3, ALU.subtract).then_inc(part("vector", step), 1)

            def d_c1(step, layer):
                dve.wait_ge(*after("scalar", ("d_c0",), layer))
                own_next(tt(e3, c3, d3, ALU.mult), layer)
                own_next(tt(row(csum), e3[:, 0, :], e3[:, 1, :], ALU.add), layer)
                own_next(tt(row(csum), row(csum), e3[:, 2, :], ALU.add), layer)
                own_next(nc.vector.reciprocal(row(csum), row(csum)), layer)
                own_next(tt(csum, csum, hrstd.unsqueeze(2).broadcast_to([P, NT, H]), ALU.mult), layer)
                tt(c3, c3, row(csum).unsqueeze(1).broadcast_to([P, GROUPS, NT * H]), ALU.mult).then_inc(part("vector", step), 1)

            def d_sum(step, layer):
                dve.wait_ge(*after("vector", ("d_c1",), layer))
                dve.wait_ge(*taken(("pv", 1, 1, 0), layer))
                for a in range(2):
                    o = og[a].rearrange("p t (h d) -> p (t h) d", h=H)
                    last = tt(o, o, per_head(c3[:, a, :], h=NT * H), ALU.mult)
                own_next(last, layer)
                tt(og[0], og[0], og[1], ALU.add).then_inc(part("vector", step), 1)

            def d_out(step, layer):
                dve.wait_ge(*after("vector", ("d_sum",), layer))
                dve.wait_ge(*after("gpsimd", step, layer))
                own_next(tt(og[0], og[0], og[2], ALU.add), layer)
                dve.wait_ge(*block_taken(unit_of("z", C), layer))
                tt(z, z, og[0], ALU.mult).then_inc(part("vector", step), 1)

            parts = {"prep": prep, **dict.fromkeys(("evict", "evict_z", "evict_first", "evict_branch"), evict), "xT": xT, "mT": mT, "latT": latT, "yT": yT_step, "dn_g0": dn_g0,
                     "dn_g1": dn_g1, "dn_gc": dn_gc, "dn_row": dn_row, "dn_fT": dn_fT, "dn_silu": dn_silu, "dn_ss": dn_ss,
                     "dn_bT": dn_bT, "dn_kk": dn_kk, "dn_qk": dn_qk, "dn_U": dn_U, "dn_TX": dn_TX, "dn_v0": dn_v0, "dn_ws": dn_ws, "dn_ds": dn_ds, "dn_o": dn_o,
                     "b_out": b_out, "q_rope": q_rope, "k_rs": k_rs, "sc": sc, "soft": soft,
                     "pv": pv, "m_out": m_out, "d_rope": d_rope, "d_c0": d_c0, "d_c1": d_c1, "d_sum": d_sum, "d_out": d_out}

            dve.wait_ge(start["pos_loaded"], 16)
            dve.wait_ge(start["tab_first"], 16)
            n_start = [0]

            def next_start(ins):
                n_start[0] += 1
                ins.then_inc(start["angle_step"], 1)
                dve.wait_ge(start["angle_step"], n_start[0])

            half = (ROPE + HD) // 2
            raw_angle = mixed[:, 1, 0:NT * half].rearrange("p (t n) -> p t n", t=NT)
            turns = [mixed[:, 1, (1 + i) * NT * half:(2 + i) * NT * half].rearrange("p (t n) -> p t n", t=NT) for i in range(2)]
            angle = [mixed[:, 0, i * NT * half:(i + 1) * NT * half].rearrange("p (t n) -> p t n", t=NT) for i in range(2)]
            next_start(nc.vector.tensor_copy(pos_f, pos_i[:, :]))
            for t in range(NT):
                last = ts(raw_angle[:, t, :], const("inv"), pos_f[:, t:t + 1], None, ALU.mult)
            next_start(last)
            for i in range(2):
                last = ts(turns[i], raw_angle, 1.0 / TWO_PI, 0.25 * i, ALU.mult, ALU.add)
            next_start(last)
            for op in (ALU.add, ALU.subtract):
                for i in range(2):
                    last = ts(turns[i], turns[i], ROUND, None, op)
                next_start(last)
            for n, part_ in enumerate(TWO_PI_PARTS):
                for i in range(2):
                    last = stt(angle[i], turns[i], -part_, angle[i] if n else raw_angle, ALU.mult, ALU.add)
                next_start(last)
            for i in range(2):
                last = ts(angle[i], angle[i], 0.5 * np.pi * i, PI_BELOW, ALU.add, ALU.min)
            next_start(last)
            for i in range(2):
                last = ts(angle[i], angle[i], -PI_BELOW, None, ALU.max)
            last.then_inc(start["angles"], 1)
            dve.wait_ge(start["rows_T"], 1)
            nc.vector.tensor_copy(prm_all[:, :], ps[7][:, 0:DEPTH * PRM_ROWS]).then_inc(start["rows_copied"], 1)
            dve.wait_ge(start["sines"], 1)
            first = {ROPE: 0, HD: ROPE // 2}
            for n in (ROPE, HD):
                for i, (o, f) in enumerate(((NT * half, 1.0), (0, 1.0))):
                    v = mixed[:, 0, o:o + NT * half].rearrange("p (t n) -> p t n", t=NT)[:, :, first[n]:first[n] + n // 2]
                    ts(rot[n][i][:, :, 0:n // 2], v, 1.0, None, ALU.mult)
                    last = ts(rot[n][i][:, :, n // 2:n], v, 1.0 if i == 0 else -1.0, None, ALU.mult)
            last.then_inc(start["rot_ready"], 1)
            dve.wait_ge(start["rows_copied"], 1)
            with dve.Fori(0, DEPTH) as layer:
                for step in ORDER:
                    if step[0] in parts:
                        parts[step[0]](step, layer)

        @block.gpsimd
        def _(pool):
            tt = nc.gpsimd.tensor_tensor

            def tc(dst, src, name, op):
                c = const(name)
                for _ in range(len(src.shape) - 2):
                    c = c.unsqueeze(1)
                return tt(dst, src, c.broadcast_to(list(src.shape)), op)

            def own_next(ins, layer):
                seen["gpsimd"] += 1
                ins.then_inc(own["gpsimd"], 1)
                pool.wait_ge(own["gpsimd"], layer * OWN["gpsimd"] + seen["gpsimd"])

            def inverse_root(dst, src, scale, layer):
                own_next(tc(dst, src, scale, ALU.mult), layer)
                own_next(tc(dst, dst, "eps", ALU.add), layer)
                return tc(dst, dst, "power", ALU.pow)

            def evict(step, layer):
                u = step[1]
                what, i, hf, nk, n = UNITS[u]
                pool.wait_ge(*block_taken(u, layer))
                m = mixed[:, :, (i % 2) * n:(i % 2 + 1) * n]
                tt(m, m, gate, ALU.add).then_inc(part("gpsimd", step), 1)

            def norm(step, layer):
                pool.wait_ge(*after("scalar", step, layer))
                own_next(inverse_root(rstd, ss_x, "inv_d", layer), layer)
                tc(hrstd, rstd, "half", ALU.mult).then_inc(part("gpsimd", step), 1)

            def tables_of(names, step, layer):
                for name in names:
                    n = ROPE if name[0] == "m" else HD
                    gn = gains(name)[:, -n:]
                    for i in range(2):
                        last = tt(rg[name][i], rot[n][i], gn.unsqueeze(1).broadcast_to([P, NT, n]), ALU.mult)
                last.then_inc(part("gpsimd", step), 1)

            def m_tables(step, layer):
                pool.wait_ge(gains_loaded, layer * (7 * 16) + 7 * 16)
                pool.wait_ge(start["rot_ready"], 1)
                tables_of(("mq", "mk"), step, layer)

            def d_tables(step, layer):
                pool.wait_ge(*after("vector", ("m_out",), layer))
                pool.wait_ge(*full(("pv", "m", 1, 0), layer))
                tables_of(("dq", "dk"), step, layer)

            def lat_norm(step, layer):
                pool.wait_ge(*after("scalar", step, layer))
                own_next(tt(lrs, lss, const("inv_n").unsqueeze(1).broadcast_to([P, NT, 3]), ALU.mult), layer)
                own_next(tc(lrs, lrs, "eps", ALU.add), layer)
                tc(lrs, lrs, "power", ALU.pow).then_inc(part("gpsimd", step), 1)

            def rotate(v, name, h, scale, t, layer):
                x, y = (gate[:, t, i * H * ROPE:(i * H + h) * ROPE].rearrange("p (h d) -> p h d", h=h) for i in range(2))
                c, s = (rg[name][i][:, t, :].unsqueeze(1).broadcast_to([P, h, ROPE]) for i in range(2))
                own_next(tt(v, v, scale, ALU.mult), layer)
                tt(x, v, c, ALU.mult)
                own_next(tt(y, v, s, ALU.mult), layer)
                n = ROPE // 2
                tt(v[:, :, 0:n], x[:, :, 0:n], y[:, :, n:ROPE], ALU.add)
                return tt(v[:, :, n:ROPE], x[:, :, n:ROPE], y[:, :, 0:n], ALU.add)

            def kpe(step, layer):
                pool.wait_ge(*after("gpsimd", ("lat_norm",), layer))
                pool.wait_ge(*layer_start(layer))
                for t in range(NT):
                    v = lat[:, t, Q_RANK + KV_RANK:].unsqueeze(1)
                    last = rotate(v, "mk", 1, per_head(lrs[:, t, 2:3], ROPE, 1), t, layer)
                last.then_inc(part("gpsimd", step), 1)

            def q_rs(step, layer):
                pool.wait_ge(*block_taken(unit_of("qb", 1), layer))
                inverse_root(hrs[:, :, 0:H], hss[:, :, 0:H], "inv_hd", layer)
                inverse_root(hrs[:, :, H:2 * H], hss[:, :, H:2 * H], "inv_rope", layer).then_inc(part("gpsimd", step), 1)

            def q_rope(step, layer):
                t = step[1]
                pool.wait_ge(*after("gpsimd", ("q_rs",), layer))
                pool.wait_ge(*after("gpsimd", ("kpe",), layer))
                v = mq[:, t, :].rearrange("p (h d) -> p h d", h=H)[:, :, HD:QK]
                rotate(v, "mq", H, per_head(hrs[:, t, H:2 * H], ROPE), t, layer).then_inc(part("gpsimd", step), 1)

            def k_rs(step, layer):
                pool.wait_ge(*block_taken(unit_of("kvb", 1), layer))
                inverse_root(hrs[:, :, 2 * H:3 * H], hss[:, :, 2 * H:3 * H], "inv_hd", layer).then_inc(part("gpsimd", step), 1)

            def dn_gc(step, layer):
                pool.wait_ge(*after("scalar", step, layer))
                pool.wait_ge(start["tab_loaded"], 16)
                tt(begc, beta, egc, ALU.mult).then_inc(part("gpsimd", step), 1)

            def dn_decay(step, layer):
                t = step[1]
                pool.wait_ge(*after("scalar", step, layer))
                own_next(tt(heads(d_D[:, t, :]), heads(d_D[:, t, :]), over_heads(const("strict")), ALU.mult), layer)
                tt(heads(d_Dt[:, t, :]), heads(d_Dt[:, t, :]), over_heads(const("tri")), ALU.mult)
                tt(heads(d_D[:, t, :]), heads(d_D[:, t, :]), per_head(beta[:, t, :]), ALU.mult).then_inc(part("gpsimd", step), 1)

            def dn_ss(step, layer):
                i = step[1]
                pool.wait_ge(*taken(step, layer))
                r = (rq, rk)[i]
                own_next(tc(r, ssd[i], "power", ALU.pow), layer)
                if i == 0:
                    own_next(tc(rq, rq, "q_scale", ALU.mult), layer)
                    pool.wait_ge(*after("scalar", ("dn_gc",), layer))
                    last = tt(rqg, rq, egc, ALU.mult)
                else:
                    tt(rkbg, rk, begc, ALU.mult)
                    last = tt(rkd, rk, edec, ALU.mult)
                last.then_inc(part("gpsimd", step), 1)

            def dn_U(step, layer):
                t = step[1]
                pool.wait_ge(*taken(step, layer))
                own_next(tt(heads(d_TT[:, t, :]), heads(d_U[:, t, :]), over_heads(const("levelT1")), ALU.mult), layer)
                tt(heads(d_TT[:, t, :]), over_heads(ident), heads(d_TT[:, t, :]), ALU.subtract).then_inc(part("gpsimd", step), 1)

            def dn_M(step, layer):
                _, s, t = step
                pool.wait_ge(*(taken(("dn_U", t), layer) if s == 1 else full(("dn_X", s - 1, t), layer)))
                tt(heads(d_Us[:, t, :]), heads(d_U[:, t, :]), over_heads(const(f"levelT{LEVELS[s]}")), ALU.mult)\
                    .then_inc(part("gpsimd", step), 1)

            def dn_dec(step, layer):
                c = step[1]
                pool.wait_ge(*taken(("dn_ds", c - 1), layer))
                e = eS[:, c // 2, (c % 2) * H:(c % 2 + 1) * H]
                tt(heads(states[c + 1]), heads(states[c]), per_head(e), ALU.mult).then_inc(part("gpsimd", step), 1)

            def dn_o(step, layer):
                t = step[1]
                pool.wait_ge(*taken(step, layer))
                tt(o_sq[:, t, :], o_sb[:, t, :], o_sb[:, t, :], ALU.mult).then_inc(part("gpsimd", step), 1)

            def dn_on(step, layer):
                pool.wait_ge(*after("vector", ("dn_o", 1), layer))
                own_next(inverse_root(ors, oss, "inv_hd", layer), layer)
                o = o_sb.rearrange("p t (h d) -> p (t h) d", h=H)
                tt(o, o, gains("dn").unsqueeze(1).broadcast_to([P, NT * H, HD]), ALU.mult)
                tt(ors, ors, hrstd.unsqueeze(2).broadcast_to([P, NT, H]), ALU.mult).then_inc(part("gpsimd", step), 1)

            def d_rs(step, layer):
                _, g, k = step
                i = 3 * g + k
                pool.wait_ge(*block_taken(unit_of("dil", i), layer))
                if g > 0:
                    pool.wait_ge(*(after("gpsimd", ("d_rope", g - 1, 1), layer) if k else after("scalar", ("soft", max(g - 2, 0), 1), layer)))
                ss, r = d_part[d_slot(i)], d_root[d_slot(i)]
                if k == 0:
                    own_next(tc(r, ss, "eps_hd", ALU.add), layer)
                    last = tc(r, r, "power", ALU.pow)
                else:
                    last = inverse_root(r, ss, "inv_hd", layer)
                last.then_inc(part("gpsimd", step), 1)

            def d_rope(step, layer):
                _, g, k = step
                pool.wait_ge(*after("vector", step, layer))
                n = HD // 2
                x = gate.rearrange("p t (h d) -> p (t h) d", h=H)
                v = stg.rearrange("p t (h d) -> p (t h) d", h=H)
                tt(x[:, :, 0:n], x[:, :, 0:n], v[:, :, n:HD], ALU.add)
                last = tt(x[:, :, n:HD], x[:, :, n:HD], v[:, :, 0:n], ALU.add)
                if k == 1:
                    own_next(last, layer)
                    for t in range(NT):
                        last = tt(heads(gate[:, t, :]), heads(gate[:, t, :]), per_head(d_root[2][:, t, :]), ALU.mult)
                last.then_inc(part("gpsimd", step), 1)

            def d_out(step, layer):
                pool.wait_ge(*after("vector", ("d_c1",), layer))
                pool.wait_ge(*taken(("pv", 2, 1, 0), layer))
                o = og[2].rearrange("p t (h d) -> p (t h) d", h=H)
                tt(o, o, per_head(cexp[:, 2].rearrange("p t h -> p (t h)"), h=NT * H), ALU.mult).then_inc(part("gpsimd", step), 1)

            parts = {"evict_branch": evict, "norm": norm, "m_tables": m_tables, "d_tables": d_tables, "lat_norm": lat_norm, "kpe": kpe,
                     "q_rs": q_rs, "q_rope": q_rope, "k_rs": k_rs, "dn_gc": dn_gc,
                     "dn_decay": dn_decay, "dn_ss": dn_ss, "dn_U": dn_U, "dn_M": dn_M,
                     "dn_dec": dn_dec, "dn_o": dn_o, "dn_on": dn_on, "d_rs": d_rs, "d_rope": d_rope, "d_out": d_out}
            pool.wait_ge(start["tab_first"], 16)
            with pool.Fori(0, DEPTH) as layer:
                for step in ORDER:
                    if step[0] in parts:
                        parts[step[0]](step, layer)

        assert seen == OWN, f"OWN = {seen}"


def kernel(**inputs):
    import concourse.bacc as bacc
    from concourse.bass_utils import run_bass_kernel_spmd

    names = ["x", "positions", "norm_g", "w_in", "mla_q_a_norm_g", "mla_w_q_b", "mla_kv_a_norm_g", "mla_w_kv_b",
             "mla_q_norm_g", "mla_k_norm_g", "dn_conv_w", "dn_a_log", "dn_dt_bias", "dn_out_norm_g",
             "dil_q_norm_g", "dil_k_norm_g", "w_branch", "w_out"]
    nc = bacc.Bacc("TRN2", target_bir_lowering=False, num_devices=1)
    arrays = {name: np.ascontiguousarray(inputs[name]) for name in names}
    arrays["tables"] = shape_tables()
    args = [nc.dram_tensor(f"in_{name}", a.shape, mybir.dt.from_np(a.dtype), kind="ExternalInput").ap() for name, a in arrays.items()]
    args.append(nc.dram_tensor("out", arrays["x"].shape, F32, kind="ExternalOutput").ap())
    hybrid_trunk(nc, *args)
    r = run_bass_kernel_spmd(nc, [{f"in_{name}": a for name, a in arrays.items()}], core_ids=[0])
    return r.results[0]["out"]
```
